# Optimizing a Trainium2 kernel written in Bass

```python
import jax, jax.numpy as jnp
from jax import lax
import numpy as np

D_MODEL = 2048
BATCH = 1
SEQ = 256
DEPTH = 2

HEAD_DIM = 64
A_Q_HEADS = D_MODEL // (2 * HEAD_DIM)
A_KV_HEADS = 2
A_WINDOW = 128
B_HEADS = D_MODEL // (2 * HEAD_DIM)
C_HEADS = D_MODEL // HEAD_DIM
C_PAIRS = ((128, 1), (512, 4), (2048, 16))
BLOCK = 128
D_FF = ((8 * D_MODEL // 3 + 255) // 256) * 256
N_EVEN = (DEPTH + 1) // 2
N_ODD = DEPTH // 2
EVEN_IN = (A_Q_HEADS + 2 * A_KV_HEADS + 3 * B_HEADS) * HEAD_DIM
EVEN_OUT = (A_Q_HEADS + B_HEADS) * HEAD_DIM
ODD_IN = 3 * C_HEADS * HEAD_DIM
ODD_OUT = C_HEADS * HEAD_DIM
RMS_EPS = 1e-6

kernel_name = 'hybrid_swa_sink_stickbreak_dilated'

def rmsnorm(x, gain):
    xf = x.astype(jnp.float32)
    y = xf * lax.rsqrt(jnp.mean(xf * xf, axis=-1, keepdims=True) + RMS_EPS)
    return (y * gain.astype(jnp.float32)).astype(x.dtype)

def alibi_slopes(n):
    return jnp.exp2(-8.0 * jnp.arange(1, n + 1, dtype=jnp.float32) / n)

def band_blocks(t):
    b, g, l, h, dh = t.shape
    nb = l // BLOCK
    tp = jnp.pad(t, ((0, 0), (0, 0), (BLOCK, 0), (0, 0), (0, 0)))
    prev = tp[:, :, :l].reshape(b, g, nb, BLOCK, h, dh)
    cur = t.reshape(b, g, nb, BLOCK, h, dh)
    return jnp.concatenate([prev, cur], axis=3)

def band_geometry(nb):
    i = jnp.arange(BLOCK)[:, None]
    j = jnp.arange(2 * BLOCK)[None, :]
    dist = i + BLOCK - j
    key_pos = jnp.arange(nb)[:, None] * BLOCK - BLOCK + jnp.arange(2 * BLOCK)[None, :]
    return dist, key_pos >= 0

def swa_sink_attention(q, k, v, sinks, slopes):
    b, s, hq, dh = q.shape
    hkv = k.shape[2]
    grp = hq // hkv
    nb = s // BLOCK
    qb = q.reshape(b, nb, BLOCK, hkv, grp, dh)
    kb = band_blocks(k[:, None])[:, 0]
    vb = band_blocks(v[:, None])[:, 0]
    sc = jnp.einsum('bnqhgd,bnkhd->bnhgqk', qb, kb).astype(jnp.float32) * dh ** -0.5
    dist, kvalid = band_geometry(nb)
    valid = (dist >= 0) & (dist < A_WINDOW) & kvalid[:, None, :]
    sc = sc - slopes.reshape(hkv, grp, 1, 1) * dist.astype(jnp.float32)
    sc = jnp.where(valid[:, None, None], sc, -jnp.inf)
    sink = sinks.astype(jnp.float32).reshape(hkv, grp)[..., None]
    m = jnp.maximum(sc.max(-1), sink)
    p = jnp.exp(sc - m[..., None])
    den = p.sum(-1) + jnp.exp(sink - m)
    o = jnp.einsum('bnhgqk,bnkhd->bnqhgd', p, vb) / jnp.moveaxis(den, -1, 2)[..., None]
    return o.reshape(b, s, hq * dh).astype(q.dtype)

def stick_breaking_attention(q, k, v):
    b, s, h, dh = q.shape
    nb = s // BLOCK
    qt = q.transpose(0, 2, 1, 3)
    kt = k.transpose(0, 2, 1, 3)
    vt = v.transpose(0, 2, 1, 3)
    key_pos = jnp.arange(s)

    def one_block(n):
        qb = lax.dynamic_slice_in_dim(qt, n * BLOCK, BLOCK, axis=2)
        z = jnp.einsum('bhqd,bhkd->bhqk', qb, kt).astype(jnp.float32) * dh ** -0.5
        q_pos = n * BLOCK + jnp.arange(BLOCK)
        causal = key_pos[None, :] < q_pos[:, None]
        log_keep = jnp.where(causal, jax.nn.log_sigmoid(-z), 0.0)
        between = lax.cumsum(log_keep, axis=3, reverse=True) - log_keep
        w = jnp.where(causal, jnp.exp(jax.nn.log_sigmoid(z) + between), 0.0)
        return jnp.einsum('bhqk,bhkd->bhqd', w, vt)

    o = lax.map(one_block, jnp.arange(nb))
    return o.transpose(1, 0, 3, 2, 4).reshape(b, s, h * dh).astype(q.dtype)

def dilated_branch(q, k, v, slopes, window, dilation):
    b, s, h, dh = q.shape
    l = s // dilation
    lp = -(-l // BLOCK) * BLOCK
    nb = lp // BLOCK

    def by_residue(t):
        t = t.reshape(b, l, dilation, h, dh).transpose(0, 2, 1, 3, 4)
        return jnp.pad(t, ((0, 0), (0, 0), (0, lp - l), (0, 0), (0, 0)))

    qb = by_residue(q).reshape(b, dilation, nb, BLOCK, h, dh)
    kb = band_blocks(by_residue(k))
    vb = band_blocks(by_residue(v))
    sc = jnp.einsum('bgnqhd,bgnkhd->bgnhqk', qb, kb).astype(jnp.float32) * dh ** -0.5
    dist, kvalid = band_geometry(nb)
    valid = (dist >= 0) & (dist <= window // dilation) & kvalid[:, None, :]
    sc = sc - slopes[:, None, None] * (dist * dilation).astype(jnp.float32)
    sc = jnp.where(valid[:, None], sc, -jnp.inf)
    m = sc.max(-1)
    p = jnp.exp(sc - m[..., None])
    den = p.sum(-1)
    num = jnp.einsum('bgnhqk,bgnkhd->bgnqhd', p, vb)

    def back(t):
        t = t.reshape((b, dilation, lp) + t.shape[4:])[:, :, :l]
        t = jnp.moveaxis(t, 1, 2)
        return t.reshape((b, s) + t.shape[3:])

    return back(num), back(jnp.moveaxis(m, -1, 3)), back(jnp.moveaxis(den, -1, 3))

def dilated_mixture(q, k, v, slopes):
    b, s, h, dh = q.shape
    branches = [dilated_branch(q, k, v, slopes, w, d) for (w, d) in C_PAIRS]
    m_all = jnp.stack([br[1] for br in branches])
    wts = jnp.exp(m_all - m_all.max(0))
    num = wts[0][..., None] * branches[0][0]
    den = wts[0] * branches[0][2]
    for idx in range(1, len(branches)):
        num = num + wts[idx][..., None] * branches[idx][0]
        den = den + wts[idx] * branches[idx][2]
    out = num / den[..., None]
    return out.reshape(b, s, h * dh).astype(q.dtype)

def swiglu(h, w_gate, w_up, w_down):
    return (jax.nn.silu(h @ w_gate) * (h @ w_up)) @ w_down

def setup_inputs(seed: int = 0) -> dict:
    key = jax.random.key(seed)
    ks = jax.random.split(key, 15)

    def normal(k, shape, scale):
        return jax.random.normal(k, shape, jnp.float32) * scale

    out_scale = (2.0 * DEPTH) ** -0.5
    return {
        'x': normal(ks[0], (BATCH, SEQ, D_MODEL), 1.0),
        'attn_norm': 1.0 + normal(ks[1], (DEPTH, D_MODEL), 0.1),
        'ffn_norm': 1.0 + normal(ks[2], (DEPTH, D_MODEL), 0.1),
        'even_w_in': normal(ks[3], (N_EVEN, D_MODEL, EVEN_IN), D_MODEL ** -0.5),
        'even_q_norm': 1.0 + normal(ks[4], (N_EVEN, HEAD_DIM), 0.1),
        'even_k_norm': 1.0 + normal(ks[5], (N_EVEN, HEAD_DIM), 0.1),
        'even_sinks': normal(ks[6], (N_EVEN, A_Q_HEADS), 0.5),
        'even_w_out': normal(ks[7], (N_EVEN, EVEN_OUT, D_MODEL), EVEN_OUT ** -0.5 * out_scale),
        'odd_w_in': normal(ks[8], (N_ODD, D_MODEL, ODD_IN), D_MODEL ** -0.5),
        'odd_q_norm': 1.0 + normal(ks[9], (N_ODD, HEAD_DIM), 0.1),
        'odd_k_norm': 1.0 + normal(ks[10], (N_ODD, HEAD_DIM), 0.1),
        'odd_w_out': normal(ks[11], (N_ODD, ODD_OUT, D_MODEL), ODD_OUT ** -0.5 * out_scale),
        'ffn_w_gate': normal(ks[12], (DEPTH, D_MODEL, D_FF), D_MODEL ** -0.5),
        'ffn_w_up': normal(ks[13], (DEPTH, D_MODEL, D_FF), D_MODEL ** -0.5),
        'ffn_w_down': normal(ks[14], (DEPTH, D_FF, D_MODEL), D_FF ** -0.5 * out_scale),
    }

def reference(x, attn_norm, ffn_norm, even_w_in, even_q_norm, even_k_norm, even_sinks,
              even_w_out, odd_w_in, odd_q_norm, odd_k_norm, odd_w_out,
              ffn_w_gate, ffn_w_up, ffn_w_down):
    b, s, _ = x.shape
    slopes_a = alibi_slopes(A_Q_HEADS)
    slopes_c = alibi_slopes(C_HEADS)
    split_even = (A_Q_HEADS * HEAD_DIM,
                  (A_Q_HEADS + A_KV_HEADS) * HEAD_DIM,
                  (A_Q_HEADS + 2 * A_KV_HEADS) * HEAD_DIM,
                  (A_Q_HEADS + 2 * A_KV_HEADS + B_HEADS) * HEAD_DIM,
                  (A_Q_HEADS + 2 * A_KV_HEADS + 2 * B_HEADS) * HEAD_DIM)
    for i in range(DEPTH):
        j = i // 2
        h = rmsnorm(x, attn_norm[i])
        if i % 2 == 0:
            proj = h @ even_w_in[j]
            qa, ka, va, qb, kb, vb = jnp.split(proj, split_even, axis=-1)
            qa = rmsnorm(qa.reshape(b, s, A_Q_HEADS, HEAD_DIM), even_q_norm[j])
            ka = rmsnorm(ka.reshape(b, s, A_KV_HEADS, HEAD_DIM), even_k_norm[j])
            va = va.reshape(b, s, A_KV_HEADS, HEAD_DIM)
            oa = swa_sink_attention(qa, ka, va, even_sinks[j], slopes_a)
            ob = stick_breaking_attention(qb.reshape(b, s, B_HEADS, HEAD_DIM),
                                          kb.reshape(b, s, B_HEADS, HEAD_DIM),
                                          vb.reshape(b, s, B_HEADS, HEAD_DIM))
            mixed = jnp.concatenate([oa, ob], axis=-1) @ even_w_out[j]
        else:
            proj = h @ odd_w_in[j]
            qc, kc, vc = jnp.split(proj, 3, axis=-1)
            qc = rmsnorm(qc.reshape(b, s, C_HEADS, HEAD_DIM), odd_q_norm[j])
            kc = rmsnorm(kc.reshape(b, s, C_HEADS, HEAD_DIM), odd_k_norm[j])
            vc = vc.reshape(b, s, C_HEADS, HEAD_DIM)
            mixed = dilated_mixture(qc, kc, vc, slopes_c) @ odd_w_out[j]
        x = x + mixed
        h = rmsnorm(x, ffn_norm[i])
        x = x + swiglu(h, ffn_w_gate[i], ffn_w_up[i], ffn_w_down[i])
    return x


_drawn_inputs = setup_inputs


def setup_inputs(seed=0):
    import zlib

    import numpy as np

    out = dict(_drawn_inputs(seed))
    spreads = {}
    factors = {'even_q_norm': 6.21,
     'even_k_norm': 5.646,
     'even_sinks': 23.683,
     'odd_q_norm': 4.162,
     'odd_k_norm': 4.096}
    for name, (base, spread) in spreads.items():
        noise = np.random.default_rng([zlib.crc32(name.encode()), seed]).standard_normal(out[name].shape)
        drawn = base * np.exp(spread * noise) if base else spread * noise
        out[name] = __import__('jax').numpy.asarray(drawn.astype(out[name].dtype))
    for name, factor in factors.items():
        out[name] = (out[name] * factor).astype(out[name].dtype)
    return out
```

```python
from contextlib import ExitStack, contextmanager

import numpy as np

import concourse.bass as bass
from concourse import mybir

F32 = mybir.dt.float32
F32R = mybir.dt.float32r
ALU = mybir.AluOpType
ACT = mybir.ActivationFunctionType
AX_X = mybir.AxisListType.X

P = 128
HD = 64
GROUP = 8
NB = 512
CHUNK = 4 * NB
HALF = CHUNK // 2
RAW = 4
SPLIT = 4
AHEAD = 3
EPS = 1e-6
NEG = -1e30
S384 = 3 * P

SLOTS24 = ([0, 2, 5, 7, 10, 12, 15, 17], 2, 4)
SLOTS20 = ([0, 2, 4, 6, 8, 10, 12, 14], 2, 4)
SLOTS16 = ([0, 1, 3, 5, 7, 9, 11, 13], 1, 2)
SLOTS12 = ([0, 1, 2, 4, 5, 6, 8, 9], 1, 2)


class Count:

    def __init__(self):
        self.c, self.per, self.i = 0, 0, None

    def past(self, n):
        return self.i is not None or self.c >= n

    def value(self, more=0, unit=1):
        at = (self.c + more) * unit
        return at if self.i is None else self.i * (self.per * unit) + at

    def slot(self, ring, more=0):
        assert self.per % ring == 0
        return (self.c + more) % ring

    def turn(self, ring, more=0, plus=0, unit=1):
        at = ((self.c + more) // ring + plus) * unit
        return at if self.i is None else self.i * (self.per // ring * unit) + at


class Counts:

    def __init__(self):
        self.half = Count()
        self.chunk = Count()
        self.x = Count()
        self.xT = Count()
        self.rms = Count()
        self.norm = Count()
        self.qkT = Count()
        self.head = Count()
        self.oT = Count()
        self.hT = Count()
        self.kt = Count()
        self.sets = [Count(), Count()]

    @contextmanager
    def loop(self, eng, rounds, sets=(0, 0), **per):
        known = {"half": self.half, "chunk": self.chunk, "norm": self.norm, "qkT": self.qkT, "head": self.head,
                 "oT": self.oT, "hT": self.hT, "kt": self.kt}
        every = [(v, per.get(k, 0)) for k, v in known.items()] + list(zip(self.sets, sets))
        start = [v.c for v, _ in every]
        with eng.Fori(0, rounds) as i:
            for v, k in every:
                v.i, v.per = (i, k) if k else (None, 0)
            yield i
            for (v, k), c in zip(every, start):
                assert v.c == c + k, (v.c, c, k)
                v.i, v.c, v.per = None, c + rounds * k, 0


def steps_at(slots, k):
    qk, mid, last = slots
    out = []
    for h in range(GROUP):
        if qk[h] + last == k:
            out.append(("pv", h))
    for h in range(GROUP):
        if qk[h] + mid == k:
            out.append(("mid", h))
    for h in range(GROUP):
        if qk[h] == k:
            out.append(("qk", h))
    return out


def make_constants(n_a, n_c):
    q = np.arange(P)[:, None]
    k = np.arange(P)[None, :]
    dist = np.concatenate([q - k, q + P - k, q - k], 1)
    in_a = (dist >= 0) & (dist < 128)
    count = (((dist >= 0) & (dist <= 128)).astype(int) + ((dist >= 0) & (dist % 4 == 0))
             + ((dist >= 0) & (dist % 16 == 0)))
    c_mask = np.where(count > 0, np.log(np.maximum(count, 1)), NEG)
    keep = np.concatenate([k > q, np.ones((P, P)), k > q], 1)
    parts = {
        "minus_dist": -np.maximum(dist, 0.0),
        "a_mask": np.where(in_a, 0.0, NEG),
        "b_keep": keep,
        "b_mask": np.where(keep > 0, 0.0, NEG),
        "ident": np.eye(P),
        "tri": np.where(q >= k, -1.0, 0.0),
        "ones": np.full((P, P), -1.0),
        "slopes": np.tile(np.concatenate([2.0 ** (-8.0 * np.arange(1, n_a + 1) / n_a),
                                          2.0 ** (-8.0 * np.arange(1, n_c + 1) / n_c)]), (P, 1)),
        "half": np.full((P, 16), -0.5),
    }
    return np.concatenate([v.astype(np.float32) for v in parts.values()], 1), \
        {n: v.shape[1] for n, v in parts.items()}, c_mask.astype(np.float32)


def decoder_kernel(nc, widths, x_in, attn_norm, ffn_norm, even_w_in, even_q_norm, even_k_norm, even_sinks,
                   even_w_out, odd_w_in, odd_q_norm, odd_k_norm, odd_w_out, w_gate, w_up, w_down,
                   consts, c_mask_in, out):
    _, SEQ, D = x_in.shape
    FF = w_gate.shape[2]
    MT = SEQ // P
    KT = D // P
    JB = D // NB
    FB = FF // NB
    FK = FF // P
    NA = even_sinks.shape[1]
    NC = D // HD
    CG = NC // GROUP
    assert MT == 2 and KT == 16 and JB == 4 and NA == 2 * GROUP and FF % NB == 0
    AQ, AK = NA * HD, 2 * HD
    OFF, at = {}, 0
    for name, width in widths.items():
        OFF[name] = at
        at += width
    CONSTS = len(widths) - 1 + 8 + 1
    HALVES = 4 + 8 * 8 + 2 * 4 * 8 + 3 * CG * 8 + 2 * (2 * FB * 8 + FK * 2)
    BQ = AQ + 2 * AK

    with ExitStack() as ctx:
        def sb(name, shape, dt, stack=ctx):
            return stack.enter_context(nc.sbuf_tensor(name, shape, dt))

        def sem(name):
            return ctx.enter_context(nc.semaphore(name))

        raw = sb("raw", [P, RAW, CHUNK], F32)
        w_hi = sb("w_hi", [P, SPLIT, HALF], F32R)
        w_lo = sb("w_lo", [P, SPLIT, HALF], F32R)
        x = sb("x", [P, MT, D], F32)
        xT_hi = sb("xT_hi", [P, KT, SEQ], F32R)
        xT_lo = sb("xT_lo", [P, KT, SEQ], F32R)
        s_buf = sb("s_buf", [P, 2, S384], F32)
        p_buf = sb("p_buf", [P, 2, S384], F32)
        t_buf = sb("t_buf", [P, 2, S384], F32)
        c = {n: sb(n, [P, w], F32) for n, w in widths.items()}
        ident = c["ident"]
        gains = sb("gains", [P, 2 * 2 * KT], F32)
        qk_gain = sb("qk_gain", [P, 4], F32)
        sinks = sb("sinks", [P, NA], F32)
        sumsq = sb("sumsq", [P, MT, JB], F32)
        msq = sb("msq", [P, MT], F32)
        rstd = sb("rstd", [P, MT], F32)
        hsum = sb("hsum", [P, MT * GROUP], F32)
        hrstd = sb("hrstd", [P, MT * GROUP], F32)
        smax = sb("smax", [P, 2, 2], F32)
        nmax = sb("nmax", [P, 2, 2], F32)
        den = sb("den", [P, 2, 2], F32)
        sink_e = sb("sink_e", [P, 2, 2], F32)
        rden = sb("rden", [P, 2, 2], F32)
        with ExitStack() as s1:
            hT = sb("hT", [P, FK, SEQ], F32, s1)
            stage_hi = sb("stage_hi", [P, 4, SEQ], F32R, s1)
            stage_lo = sb("stage_lo", [P, 4, SEQ], F32R, s1)
            silu_g = sb("silu_g", [P, MT, NB], F32, s1)
            hid = sb("hid", [P, MT, NB], F32, s1)
        oT_hi = sb("oT_hi", [P, KT, SEQ], F32R)
        oT_lo = sb("oT_lo", [P, KT, SEQ], F32R)
        q_nat = sb("q_nat", [P, MT, NB], F32)
        k_nat = sb("k_nat", [P, MT, NB], F32)
        v_nat = sb("v_nat", [P, MT, NB], F32)
        qT = sb("qT", [P, 4, SEQ], F32)
        kT = sb("kT", [P, 4, SEQ], F32)
        sq = sb("sq", [P, MT, NB], F32)
        o_nat = sb("o_nat", [P, MT, NB], F32)

        acc = [ctx.enter_context(nc.psum_tensor(f"acc{i}", [P, NB], F32)) for i in range(4)]
        work = [ctx.enter_context(nc.psum_tensor(f"work{i}", [P, NB], F32)) for i in range(4)]
        down_bank = [work[0:2], acc[0:2], work[2:4], acc[2:4]]

        raw_loaded = [sem(f"raw_loaded{i}") for i in range(RAW)]
        const_loaded = sem("const_loaded")
        x_loaded = [sem(f"x_loaded{j}") for j in range(JB)]
        gain_loaded = sem("gain_loaded")
        mask_loaded = sem("mask_loaded")
        hi_ready = sem("hi_ready")
        lo_ready = sem("lo_ready")
        half_used = sem("half_used")
        acc_free = [sem(f"acc_free{i}") for i in range(2)]
        gainT_done = sem("gainT_done")
        gains_ready = sem("gains_ready")
        x_ready = sem("x_ready")
        xT_done = sem("xT_done")
        xhi_ready = sem("xhi_ready")
        xT_ready = sem("xT_ready")
        sumsq_ready = sem("sumsq_ready")
        msq_ready = sem("msq_ready")
        rstd_ready = sem("rstd_ready")
        hsum_ready = sem("hsum_ready")
        hrstd_ready = sem("hrstd_ready")
        normed = sem("normed")
        qkT_done = sem("qkT_done")
        qkT_ready = sem("qkT_ready")
        s_done = sem("s_done")
        s_ready = sem("s_ready")
        mid_done = sem("mid_done")
        pt_ready = sem("pt_ready")
        log_ready = sem("log_ready")
        mid_ready = sem("mid_ready")
        o_done = sem("o_done")
        o_ready = sem("o_ready")
        oT_done = sem("oT_done")
        ohi_ready = sem("ohi_ready")
        oT_ready = sem("oT_ready")
        hT_done = sem("hT_done")
        hT_ready = sem("hT_ready")
        shi_ready = sem("shi_ready")
        slo_ready = sem("slo_ready")
        abs_ready = sem("abs_ready")
        exp_ready = sem("exp_ready")
        sum_made = sem("sum_made")
        sq_made = sem("sq_made")
        hsum_made = sem("hsum_made")
        dist_added = sem("dist_added")
        max_made = sem("max_made")
        den_made = sem("den_made")
        rden_made = sem("rden_made")
        sp_made = sem("sp_made")
        qgain_made = sem("qgain_made")
        stored = sem("stored")

        def heads_view(t):
            return t.rearrange("p m (h d) -> p (m h) d", d=HD)

        k_dup = k_nat[:, 0, :].rearrange("p (m n) -> p m n", m=MT)

        def taken_out(eng, n):
            eng.wait_ge(acc_free[0], n.sets[0].value())
            if n.sets[1].past(1):
                eng.wait_ge(acc_free[1], n.sets[1].value())

        def walk(eng, e):
            n = Counts()
            e.n = n

            def half(**what):
                e.half(**what)
                n.half.c += 1

            def evacuate(dst, acc_set, scaled=True):
                e.evacuate(dst, acc_set)
                n.sets[acc_set].c += 1

            def xT(gain, j, needs=None):
                e.xT(gain, j, needs)
                n.xT.c += 1

            def norm_a(t):
                e.norm_a(t)

            def norm_b(t):
                e.norm_b(t)
                n.norm.c += 1

            def qkT(src, dst, gain):
                e.qkT(src, dst, gain)
                n.qkT.c += 1

            def oT(kt0):
                e.oT(kt0)
                n.oT.c += 1

            def attend(slots, k, kind, layer_c=None, kv=None):
                for what, h in steps_at(slots, k):
                    e.attend(what, h, kind, layer_c, kv)
                if k == slots[0][-1] + slots[2]:
                    n.head.c += GROUP

            def block(acc_set, src=(xT_hi, xT_lo), extra=None, first=False, added=None):
                x0 = n.xT.c // JB * JB if n.xT.c % JB else n.xT.c - JB
                for k in range(8):
                    half(src=src, kts=(2 * k, 2 * k + 1), acc_set=acc_set, start=k == 0, stop=k == 7,
                         needs=(xT_ready, x0 + k // 2 + 1) if first else None, added=added)
                    if extra:
                        extra(k)

            def residual(banks):
                e.residual(banks)
                n.x.c += 1

            def rms():
                for j in range(JB):
                    e.squares(j)
                e.rms()
                n.rms.c += 1

            def out_projection(gain, kind, layer_c, first_oT=None):
                src = (oT_hi, oT_lo)
                o0 = n.oT.c // 4 * 4
                k = 0
                for b in range(2):
                    for cc in range(6):
                        half(src=src, kts=(2 * cc, 2 * cc + 1), acc_set=b, start=cc == 0, stop=False,
                             needs=(oT_ready, o0 + cc // 2 + 1))
                        if k == 0 and first_oT is not None:
                            oT(first_oT)
                        attend(SLOTS12, k, kind, layer_c)
                        k += 1
                oT(3 * 4)
                for b in range(2):
                    for cc in (6, 7):
                        half(src=src, kts=(2 * cc, 2 * cc + 1), acc_set=b, start=False, stop=cc == 7,
                             needs=(oT_ready, o0 + 4))
                    residual(acc[2 * b:2 * b + 2])
                x0 = n.x.c - 2
                block(0, src, lambda k: xT(gain, 0, x0 + 1) if k == 2 else xT(gain, 1, x0 + 2) if k == 4 else None,
                      added=x0 + 1)
                residual(acc[0:2])
                block(1, src, lambda k: xT(gain, 2, x0 + 3) if k == 2 else None, added=x0 + 2)
                residual(acc[2:4])

            def feed_forward(layer, last):
                x0 = n.x.c
                block(0, extra=lambda k: xT(2 + layer, 3, x0) if k == 1 else None, first=True,
                      added=x0 - 1)
                rms()
                e.gate(0)
                n.sets[0].c += 1
                block(1, added=x0)
                e.up(1)
                n.sets[1].c += 1

                def hidden(j):
                    e.hidden(j)
                    n.hT.c += 1

                with n.loop(eng, FB - 1, half=16, sets=(1, 1), hT=1) as j:
                    block(0, extra=lambda k: hidden(j) if k == 2 else None)
                    e.gate(0)
                    n.sets[0].c += 1
                    block(1)
                    e.up(1)
                    n.sets[1].c += 1

                def four(at, start=False, stop=False):
                    for t in range(4):
                        e.stage(at, t)
                        n.kt.c += 1
                        for h in range(2):
                            half(down=h, stage=t, start=start and t == 0, stop=stop and t == 3)
                            if start and t == 0 and h == 0:
                                hidden(FB - 1)
                four(0, start=True)
                with n.loop(eng, FK // 4 - 2, half=8, kt=4) as j:
                    four(j * 4 + 4)
                four(FK - 4, stop=True)

            e.begin()
            xT(0, 0)
            for k in range(4):
                if k < 3:
                    xT(0, k + 1)
                half(src=(xT_hi, xT_lo), kts=range(4 * k, 4 * k + 4), acc_set=0, start=k == 0, stop=k == 3,
                     width=2 * P, needs=(xT_ready, k + 1))
            rms()
            e.evacuate_kv()
            n.sets[0].c += 1
            block(1, extra=lambda k: norm_a(k_dup) if k == 1 else norm_b(k_dup) if k == 3 else None)
            evacuate(q_nat, 1)

            def a1(k):
                if k == 0:
                    norm_a(q_nat)
                if k == 2:
                    norm_b(q_nat)
                if k == 3:
                    qkT(k_dup, kT, 1)
                    qkT(q_nat, qT, 0)
                if k >= 4:
                    attend(SLOTS16, k - 4, "soft", 0, 0)
            block(0, extra=a1)
            evacuate(q_nat, 0)

            def a2(k):
                attend(SLOTS16, k + 4, "soft", 0, 0)
                if k == 1:
                    norm_a(q_nat)
                if k == 3:
                    norm_b(q_nat)
            block(1, extra=a2)

            def a3(k):
                if k < 4:
                    attend(SLOTS16, k + 12, "soft", 0, 0)
                if k == 3:
                    qkT(q_nat, qT, 0)
                    evacuate(q_nat, 1)
                if k == 4:
                    oT(0)
                if k >= 4:
                    attend(SLOTS16, k - 4, "soft", GROUP, 1)
            block(0, extra=a3)
            evacuate(k_nat, 0)
            block(1, extra=lambda k: attend(SLOTS16, k + 4, "soft", GROUP, 1))

            def b1(k):
                if k < 4:
                    attend(SLOTS16, k + 12, "soft", GROUP, 1)
                if k == 3:
                    evacuate(v_nat, 1)
                    qkT(q_nat, qT, None)
                    qkT(k_nat, kT, False)
                if k == 4:
                    oT(4)
                if k >= 4:
                    attend(SLOTS20, k - 4, "stick")
            block(0, extra=b1)
            evacuate(q_nat, 0)
            block(1, extra=lambda k: attend(SLOTS20, k + 4, "stick"))
            evacuate(k_nat, 1)
            block(0, extra=lambda k: attend(SLOTS20, k + 12, "stick"))
            evacuate(v_nat, 0)
            qkT(q_nat, qT, None)
            qkT(k_nat, kT, False)
            out_projection(2, "stick", None, first_oT=8)
            feed_forward(0, False)

            def after_down(gain):
                x0 = n.x.c
                residual(down_bank[0])
                residual(down_bank[1])
                xT(gain, 0, x0 + 1)
                residual(down_bank[2])
                residual(down_bank[3])
                xT(gain, 1, x0 + 3)
                return lambda k: (xT(gain, 2, x0 + 4) if k == 1 else xT(gain, 3, x0 + 4) if k == 3 else None)

            block(0, extra=after_down(1), first=True)
            rms()
            evacuate(q_nat, 0)
            block(1, extra=lambda k: norm_a(q_nat) if k == 1 else norm_b(q_nat) if k == 3 else None)
            evacuate(k_nat, 1)
            block(0, extra=lambda k: norm_a(k_nat) if k == 1 else norm_b(k_nat) if k == 3 else None)
            evacuate(v_nat, 0)
            qkT(q_nat, qT, 2)
            qkT(k_nat, kT, 3)
            with n.loop(eng, CG - 1, half=24, norm=2, qkT=2, head=GROUP, oT=1, sets=(2, 1)) as g:
                slope0 = g * GROUP + NA
                block(0, extra=lambda k: attend(SLOTS24, k, "soft", slope0))
                evacuate(q_nat, 0)

                def c2(k):
                    attend(SLOTS24, k + 8, "soft", slope0)
                    if k == 1:
                        norm_a(q_nat)
                    if k == 3:
                        norm_b(q_nat)
                block(1, extra=c2)
                evacuate(k_nat, 1)

                def c3(k):
                    attend(SLOTS24, k + 16, "soft", slope0)
                    if k == 1:
                        norm_a(k_nat)
                    if k == 3:
                        norm_b(k_nat)
                    if k == 6:
                        oT(g * 4)
                block(0, extra=c3)
                evacuate(v_nat, 0)
                qkT(q_nat, qT, 2)
                qkT(k_nat, kT, 3)
            out_projection(3, "soft", NA + (CG - 1) * GROUP)
            feed_forward(1, True)
            for j in range(JB):
                residual(down_bank[j])

        def nothing(*args, **named):
            return None

        class Steps:

            def __init__(self, begin=nothing, half=nothing, evacuate=nothing, evacuate_kv=nothing, xT=nothing,
                         norm_a=nothing, norm_b=nothing, qkT=nothing, oT=nothing, attend=nothing, residual=nothing,
                         squares=nothing, rms=nothing, gate=nothing, up=nothing, hidden=nothing, stage=nothing):
                self.n = None
                self.begin, self.half, self.evacuate, self.evacuate_kv = begin, half, evacuate, evacuate_kv
                self.xT, self.norm_a, self.norm_b, self.qkT, self.oT = xT, norm_a, norm_b, qkT, oT
                self.attend, self.residual, self.squares, self.rms = attend, residual, squares, rms
                self.gate, self.up, self.hidden, self.stage = gate, up, hidden, stage

        block = ctx.enter_context(nc.Block())

        @block.sync
        def _(sp):
            n = Counts()

            def chunk(src, tiles=None):
                if n.chunk.past(RAW):
                    sp.wait_ge(lo_ready, n.chunk.value(1 - RAW, unit=2))
                s = n.chunk.slot(RAW)
                dst = raw[:, s, :]
                if tiles:
                    dst = dst.rearrange("p (t n) -> p t n", t=tiles)
                sp.dma_start(dst, src).then_inc(raw_loaded[s], 16)
                n.chunk.c += 1

            def columns(w, cols, which=range(KT // 4)):
                wv = w.rearrange("(c t p) n -> c p t n", t=4, p=P)
                for k in which:
                    chunk(wv[k][:, :, cols], 4)

            def out_projection(w):
                for cols, which in ((0, range(3)), (1, range(3)), (0, [3]), (1, [3]), (2, range(4)), (3, range(4))):
                    columns(w, slice(cols * NB, (cols + 1) * NB), which)

            def feed_forward(layer):
                with n.loop(sp, FB, chunk=8) as j:
                    columns(w_gate[layer], bass.ds(j * NB, NB))
                    columns(w_up[layer], bass.ds(j * NB, NB))
                with n.loop(sp, FK // 4, chunk=4) as j:
                    for t in range(4):
                        chunk(w_down[layer][bass.ds(j * (4 * P) + t * P, P), :])

            for j in range(JB):
                for m in range(MT):
                    sp.dma_start(x[:, m, j * NB:(j + 1) * NB],
                                 x_in[0, m * P:(m + 1) * P, j * NB:(j + 1) * NB]).then_inc(x_loaded[j], 16)
            kv = even_w_in[0].rearrange("(c t p) n -> c p t n", t=8, p=P)
            for k in range(2):
                chunk(kv[k][:, :, AQ:AQ + 2 * AK], 8)
            for first in [0, NB] + [BQ + t * AQ + g * NB for g in range(2) for t in range(3)]:
                columns(even_w_in[0], slice(first, first + NB))
            out_projection(even_w_out[0])
            feed_forward(0)
            sp.wait_ge(s_ready, 2 * GROUP)
            sp.dma_start(c["a_mask"][:, :], c_mask_in).then_inc(mask_loaded, 16)
            with n.loop(sp, CG, chunk=12) as g:
                for t in range(3):
                    columns(odd_w_in[0], bass.ds(g * NB + t * D, NB))
            out_projection(odd_w_out[0])
            feed_forward(1)
            for j in range(JB):
                sp.wait_ge(x_ready, 3 * JB + j + 1)
                for m in range(MT):
                    sp.dma_start(out[0, m * P:(m + 1) * P, j * NB:(j + 1) * NB],
                                 x[:, m, j * NB:(j + 1) * NB]).then_inc(stored, 16)
            sp.wait_ge(stored, 16 * JB * MT)

        @block.gpsimd
        def _(pool):
            def begin():
                pool.wait_ge(const_loaded, 16 * CONSTS)

            def rms():
                pool.wait_ge(msq_ready, e.n.rms.value(1))
                pool.tensor_tensor(rstd[:, :], msq[:, :], c["half"][:, 0:MT], ALU.pow).then_inc(rstd_ready, 1)

            def norm_b(t):
                pool.wait_ge(hsum_ready, e.n.norm.value(1))
                w = GROUP if t is k_dup else MT * GROUP
                pool.tensor_tensor(hrstd[:, 0:w], hsum[:, 0:w], c["half"][:, 0:w], ALU.pow).then_inc(hrstd_ready, 1)

            e = Steps(begin=begin, rms=rms, norm_b=norm_b)
            walk(pool, e)

        @block.scalar
        def _(act):
            def split(more):
                n = e.n
                if n.half.i is None and n.half.c + more >= HALVES:
                    return
                s, r = n.half.slot(SPLIT, more), n.half.slot(2 * RAW, more)
                act.wait_ge(raw_loaded[r // 2], n.half.turn(2 * RAW, more, plus=1, unit=16))
                if n.half.i is not None or n.half.c + more >= SPLIT:
                    act.wait_ge(half_used, n.half.value(more + 1 - SPLIT))
                act.activation(w_hi[:, s, :], raw[:, r // 2, (r % 2) * HALF:(r % 2 + 1) * HALF],
                               ACT.Copy).then_inc(hi_ready, 1)

            def begin():
                act.dma_start(ident[:, :], consts[:, OFF["ident"]:OFF["ident"] + P]).then_inc(gain_loaded, 16)
                for r, g in ((0, attn_norm), (2 * KT, ffn_norm)):
                    act.dma_start(s_buf[r:r + 2 * KT, 0, 0:P],
                                  g.rearrange("l (t p) -> (l t) p", p=P)).then_inc(gain_loaded, 16)
                for name in widths:
                    if name != "ident":
                        act.dma_start(c[name][:, :],
                                      consts[:, OFF[name]:OFF[name] + widths[name]]).then_inc(const_loaded, 16)
                for col, g in enumerate((even_q_norm, even_k_norm, odd_q_norm, odd_k_norm)):
                    for r in range(2):
                        act.dma_start(qk_gain[r * HD:(r + 1) * HD, col:col + 1],
                                      g.rearrange("a d -> d a")).then_inc(const_loaded, 16)
                act.dma_start(sinks[:, :], even_sinks[0:1, :].broadcast_to([P, NA])).then_inc(const_loaded, 16)
                act.wait_ge(gainT_done, 1)
                act.activation(gains[:, :], work[3][:, 0:4 * KT], ACT.Copy).then_inc(gains_ready, 1)
                act.wait_ge(gains_ready, 1)
                for k in range(AHEAD):
                    split(k)

            def evacuate(dst, acc_set):
                n = e.n
                act.wait_ge(half_used, n.half.value())
                act.wait_ge(rstd_ready, n.rms.value())
                if dst is v_nat:
                    act.wait_ge(o_done, n.head.value())
                elif n.qkT.past(1):
                    act.wait_ge(qkT_done, n.qkT.value())
                for m in range(MT):
                    last = act.activation(dst[:, m, :], acc[2 * acc_set + m][:, :], ACT.Copy, scale=rstd[:, m:m + 1])
                last.then_inc(acc_free[acc_set], 1)

            def evacuate_kv():
                act.wait_ge(half_used, e.n.half.value())
                act.wait_ge(rstd_ready, 1)
                for m in range(MT):
                    for g in range(2):
                        for r in range(2):
                            act.activation(k_dup[:, m, (2 * g + r) * HD:(2 * g + r + 1) * HD],
                                           acc[m][:, g * HD:(g + 1) * HD], ACT.Copy, scale=rstd[:, m:m + 1])
                    last = act.activation(v_nat[:, m, 0:AK], acc[m][:, AK:2 * AK], ACT.Copy, scale=rstd[:, m:m + 1])
                last.then_inc(acc_free[0], 1)

            def xT_high(gain, j, needs):
                act.wait_ge(xT_done, e.n.xT.value(1))
                for t in range(4):
                    kt = 4 * j + t
                    last = act.activation(xT_hi[:, kt, :],
                                          work[2 * (j % 2) + t // 2][:, (t % 2) * SEQ:(t % 2 + 1) * SEQ],
                                          ACT.Copy, scale=gains[:, gain * KT + kt:gain * KT + kt + 1])
                last.then_inc(xhi_ready, 1)

            def squares(j):
                n = e.n
                if n.rms.c == 0:
                    act.wait_ge(x_loaded[j], 32)
                else:
                    act.wait_ge(x_ready, n.x.c - JB + j + 1)
                if n.rms.c or j:
                    act.wait_ge(sumsq_ready, n.rms.c * JB + j)
                for m in range(MT):
                    waste = (t_buf, p_buf)[m][:, :, :].rearrange("p a b -> p (a b)")[:, 0:NB]
                    last = act.activation(waste, x[:, m, j * NB:(j + 1) * NB], ACT.Square,
                                          accum_out=sumsq[:, m, j:j + 1])
                last.then_inc(sumsq_ready, 1)

            def qkT(src, dst, gain):
                act.wait_ge(qkT_done, e.n.qkT.value(1))
                if e.n.qkT.c == 0 and e.n.qkT.i is None:
                    act.wait_ge(qgain_made, 1)
                banks = work[2:4] if dst is kT else work[0:2]
                if src is k_dup:
                    banks = banks[0:1]
                scale = qk_gain[:, gain:gain + 1] if gain is not None and gain is not False else (
                    HD ** -0.5 if gain is None else 1.0)
                for b, bank in enumerate(banks):
                    last = act.activation(dst[:, 2 * b:2 * b + 2, :].rearrange("p a b -> p (a b)"), bank[:, :],
                                          ACT.Copy, scale=scale)
                last.then_inc(qkT_ready, 1)

            def oT(kt0):
                act.wait_ge(oT_done, e.n.oT.value(1))
                for b in range(2):
                    last = act.activation(oT_hi[:, bass.ds(kt0 + 2 * b, 2), :].rearrange("p a b -> p (a b)"),
                                          work[2 + b][:, :], ACT.Copy)
                last.then_inc(ohi_ready, 1)

            def attend(what, h, kind, slope, kv):
                n, b = e.n, h % 2
                head = n.head.value(h + 1)
                if (what, kind) == ("qk", "soft"):
                    act.wait_ge(s_ready, head)
                    for m, (lo, hi) in enumerate(((0, P), (P, S384))):
                        last = act.activation(p_buf[:, b, lo:hi], s_buf[:, b, lo:hi], ACT.Exp,
                                              bias=nmax[:, b, m:m + 1], accum_out=den[:, b, m:m + 1])
                    if kv is not None:
                        last = act.activation(sink_e[:, b, :], nmax[:, b, :], ACT.Exp,
                                              bias=sinks[:, slope + h:slope + h + 1])
                    last.then_inc(mid_ready, 1)
                if (what, kind) == ("mid", "soft"):
                    act.wait_ge(mid_done, head)
                    if n.head.past(2) or h >= 2:
                        act.wait_ge(o_done, n.head.value(h - 1))
                    act.activation(t_buf[:, b, :], work[2 + b][:, 0:S384], ACT.Copy).then_inc(pt_ready, 1)
                if (what, kind) == ("qk", "stick"):
                    act.wait_ge(s_done, head)
                    k = head - NA
                    act.activation(s_buf[:, b, :], work[h % 4][:, 0:S384], ACT.Abs).then_inc(abs_ready, 1)
                    act.wait_ge(abs_ready, k)
                    act.activation(s_buf[:, b, :], s_buf[:, b, :], ACT.Exp, scale=-1.0).then_inc(exp_ready, 1)
                    act.wait_ge(exp_ready, k)
                    act.activation(s_buf[:, b, :], s_buf[:, b, :], ACT.Ln, bias=1.0).then_inc(log_ready, 1)
                if (what, kind) == ("mid", "stick"):
                    act.wait_ge(s_ready, head)
                    act.wait_ge(o_done, n.head.value(h - 1))
                    act.activation(p_buf[:, b, :], s_buf[:, b, :], ACT.Exp).then_inc(pt_ready, 1)

            def gate(acc_set):
                n = e.n
                act.wait_ge(half_used, n.half.value())
                act.wait_ge(rstd_ready, n.rms.value())
                if n.sets[1].past(1):
                    act.wait_ge(acc_free[1], n.sets[1].value())
                for m in range(MT):
                    last = act.activation(silu_g[:, m, :], acc[2 * acc_set + m][:, :], ACT.Silu,
                                          scale=rstd[:, m:m + 1])
                last.then_inc(acc_free[acc_set], 1)

            def hidden(j):
                act.wait_ge(hT_done, e.n.hT.value(1))
                for b in range(2):
                    last = act.activation(hT[:, bass.ds(j * 4 + 2 * b, 2), :].rearrange("p a b -> p (a b)"),
                                          work[2 + b][:, :], ACT.Copy)
                last.then_inc(hT_ready, 1)

            def stage(kt, t):
                n = e.n
                act.wait_ge(hT_ready, n.hT.value())
                if n.kt.past(4):
                    act.wait_ge(half_used, n.half.value(-6))
                act.activation(stage_hi[:, t, :], hT[:, kt + t, :] if isinstance(kt, int) else
                               hT[:, bass.ds(kt + t, 1), :].rearrange("p a b -> p (a b)"),
                               ACT.Copy).then_inc(shi_ready, 1)

            e = Steps(begin=begin, half=lambda **w: split(AHEAD), evacuate=evacuate, evacuate_kv=evacuate_kv,
                      xT=xT_high, squares=squares, qkT=qkT, oT=oT, attend=attend, gate=gate, hidden=hidden,
                      stage=stage)
            walk(act, e)

        @block.vector
        def _(dve):
            def split(more):
                n = e.n
                if n.half.i is None and n.half.c + more >= HALVES:
                    return
                s, r = n.half.slot(SPLIT, more), n.half.slot(2 * RAW, more)
                dve.wait_ge(hi_ready, n.half.value(more + 1))
                dve.tensor_tensor(w_lo[:, s, :], raw[:, r // 2, (r % 2) * HALF:(r % 2 + 1) * HALF],
                                  w_hi[:, s, :].bitcast(F32), ALU.subtract).then_inc(lo_ready, 1)

            def begin():
                for k in range(AHEAD):
                    split(k)

            def evacuate_kv():
                dve.wait_ge(const_loaded, 16 * CONSTS)
                for col in (0, 2):
                    last = dve.tensor_scalar(qk_gain[:, col:col + 1], qk_gain[:, col:col + 1], HD ** -0.5, None,
                                             ALU.mult)
                last.then_inc(qgain_made, 1)

            def xT_low(gain, j, needs):
                dve.wait_ge(xhi_ready, e.n.xT.value(1))
                for t in range(4):
                    kt = 4 * j + t
                    last = dve.scalar_tensor_tensor(
                        out=xT_lo[:, kt, :], in0=work[2 * (j % 2) + t // 2][:, (t % 2) * SEQ:(t % 2 + 1) * SEQ],
                        scalar=gains[:, gain * KT + kt:gain * KT + kt + 1], in1=xT_hi[:, kt, :].bitcast(F32),
                        op0=ALU.mult, op1=ALU.subtract)
                last.then_inc(xT_ready, 1)

            def rms():
                k = e.n.rms.value(1)
                dve.wait_ge(sumsq_ready, k * JB)
                dve.tensor_reduce(msq[:, :], sumsq[:, :, :], AX_X, ALU.add).then_inc(sum_made, 1)
                dve.wait_ge(sum_made, k)
                dve.tensor_scalar(msq[:, :], msq[:, :], 1.0 / D, EPS, ALU.mult, ALU.add).then_inc(msq_ready, 1)

            def norm_a(t):
                k = e.n.norm.value(1)
                v = heads_view(t)
                w = v.shape[1]
                sqv = sq[:, :, :].rearrange("p m n -> p (m n)")[:, 0:w * HD].rearrange("p (h d) -> p h d", d=HD)
                taken_out(dve, e.n)
                dve.tensor_tensor(sqv, v, v, ALU.mult).then_inc(sq_made, 1)
                dve.wait_ge(sq_made, k)
                dve.tensor_reduce(hsum[:, 0:w], sqv, AX_X, ALU.add).then_inc(hsum_made, 1)
                dve.wait_ge(hsum_made, k)
                dve.tensor_scalar(hsum[:, 0:w], hsum[:, 0:w], 1.0 / HD, EPS, ALU.mult, ALU.add).then_inc(hsum_ready, 1)

            def norm_b(t):
                v = heads_view(t)
                w = v.shape[1]
                dve.wait_ge(hrstd_ready, e.n.norm.value(1))
                dve.tensor_tensor(v, v, hrstd[:, 0:w].unsqueeze(2).broadcast_to([P, w, HD]),
                                  ALU.mult).then_inc(normed, 1)

            def oT(kt0):
                dve.wait_ge(ohi_ready, e.n.oT.value(1))
                for b in range(2):
                    at = bass.ds(kt0 + 2 * b, 2)
                    last = dve.tensor_tensor(oT_lo[:, at, :].rearrange("p a b -> p (a b)"), work[2 + b][:, :],
                                             oT_hi[:, at, :].rearrange("p a b -> p (a b)").bitcast(F32), ALU.subtract)
                last.then_inc(oT_ready, 1)

            def attend(what, h, kind, slope, kv):
                n, b = e.n, h % 2
                head = n.head.value(h + 1)
                if (what, kind) == ("qk", "soft"):
                    at = bass.ds(slope + h, 1)
                    dve.wait_ge(s_done, head)
                    dve.scalar_tensor_tensor(out=s_buf[:, b, :], in0=c["minus_dist"][:, :], scalar=c["slopes"][:, at],
                                             in1=work[b][:, 0:S384], op0=ALU.mult, op1=ALU.add).then_inc(dist_added, 1)
                    soft = head if kv is not None else head - NA
                    if kv is None:
                        dve.wait_ge(mask_loaded, 16)
                    dve.wait_ge(dist_added, soft)
                    dve.nop(nofuse=True)
                    for m, (lo, hi) in enumerate(((0, P), (P, S384))):
                        last = dve.tensor_tensor_reduce(s_buf[:, b, lo:hi], s_buf[:, b, lo:hi], c["a_mask"][:, lo:hi],
                                                        1.0, -3e38, ALU.add, ALU.max, smax[:, b, m:m + 1])
                    last.then_inc(max_made, 1)
                    dve.wait_ge(max_made, soft)
                    floor = -3e38 if kv is None else sinks[:, slope + h:slope + h + 1]
                    dve.tensor_scalar(nmax[:, b, :], smax[:, b, :], floor, -1.0, ALU.max, ALU.mult).then_inc(s_ready, 1)
                if (what, kind) == ("qk", "stick"):
                    dve.wait_ge(log_ready, head - NA)
                    dve.scalar_tensor_tensor(out=t_buf[:, b, :], in0=work[h % 4][:, 0:S384], scalar=0.0,
                                             in1=s_buf[:, b, :], op0=ALU.max, op1=ALU.add).then_inc(sp_made, 1)
                    dve.wait_ge(sp_made, head - NA)
                    dve.tensor_tensor(t_buf[:, b, :], t_buf[:, b, :], c["b_keep"][:, :],
                                      ALU.mult).then_inc(mid_ready, 1)
                if (what, kind) == ("mid", "stick"):
                    dve.wait_ge(mid_done, head)
                    dve.tensor_tensor(s_buf[:, b, :], work[h % 4][:, 0:S384], c["b_mask"][:, :],
                                      ALU.add).then_inc(s_ready, 1)
                if what == "pv":
                    dve.wait_ge(o_done, head)
                    o = o_nat[:, :, h * HD:(h + 1) * HD]
                    bank = work[2 + b] if kind == "soft" else work[h % 4]
                    src = bank[:, S384:NB].rearrange("p (m d) -> p m d", m=MT)
                if (what, kind) == ("pv", "soft"):
                    if kv is not None:
                        dve.tensor_tensor(den[:, b, :], den[:, b, :], sink_e[:, b, :], ALU.add).then_inc(den_made, 1)
                        dve.wait_ge(den_made, head)
                    dve.reciprocal(rden[:, b, :], den[:, b, :]).then_inc(rden_made, 1)
                    dve.wait_ge(rden_made, head if kv is not None else head - NA)
                    dve.tensor_tensor(o, src, rden[:, b, :].unsqueeze(2).broadcast_to([P, MT, HD]),
                                      ALU.mult).then_inc(o_ready, 1)
                if (what, kind) == ("pv", "stick"):
                    dve.tensor_copy(o, src).then_inc(o_ready, 1)

            def residual(banks):
                n = e.n
                j = n.x.c % JB
                dve.wait_ge(half_used, n.half.value())
                dve.wait_ge(sumsq_ready, n.rms.value(unit=JB))
                for m in range(MT):
                    xs = x[:, m, j * NB:(j + 1) * NB]
                    last = dve.tensor_tensor(xs, banks[m][:, :], xs, ALU.add)
                last.then_inc(x_ready, 1)

            def up(acc_set):
                n = e.n
                dve.wait_ge(half_used, n.half.value())
                dve.wait_ge(acc_free[0], n.sets[0].value())
                if n.hT.past(1):
                    dve.wait_ge(hT_done, n.hT.value())
                for m in range(MT):
                    last = dve.scalar_tensor_tensor(out=hid[:, m, :], in0=acc[2 * acc_set + m][:, :],
                                                    scalar=rstd[:, m:m + 1], in1=silu_g[:, m, :],
                                                    op0=ALU.mult, op1=ALU.mult)
                last.then_inc(acc_free[acc_set], 1)

            def stage(kt, t):
                dve.wait_ge(shi_ready, e.n.kt.value(1))
                dve.tensor_tensor(stage_lo[:, t, :], hT[:, bass.ds(kt + t, 1), :].rearrange("p a b -> p (a b)"),
                                  stage_hi[:, t, :].bitcast(F32), ALU.subtract).then_inc(slo_ready, 1)

            e = Steps(begin=begin, half=lambda **w: split(AHEAD), evacuate_kv=evacuate_kv, xT=xT_low, rms=rms, norm_a=norm_a, norm_b=norm_b,
                      oT=oT, attend=attend, residual=residual, up=up, stage=stage)
            walk(dve, e)

        @block.tensor
        def _(pe):
            def begin():
                pe.wait_ge(gain_loaded, 16 * 3)
                pe.transpose(work[3][:, 0:4 * KT], s_buf[0:4 * KT, 0, 0:P], ident[0:4 * KT, 0:4 * KT]).then_inc(gainT_done, 1)

            def three(out_ps, x_hi, x_lo, wh, wl, start, stop):
                pe.matmul(out_ps, x_hi, wh, start=start, stop=False)
                pe.matmul(out_ps, x_hi, wl, start=False, stop=False)
                return pe.matmul(out_ps, x_lo, wh, start=False, stop=stop)

            def half(src=None, kts=None, acc_set=None, start=False, stop=False, width=NB, needs=None,
                     added=None, down=None, stage=None):
                n = e.n
                s = n.half.slot(SPLIT)
                pe.wait_ge(lo_ready, n.half.value(1))
                if down is None:
                    if start and n.sets[acc_set].past(1):
                        pe.wait_ge(acc_free[acc_set], n.sets[acc_set].value())
                    if start and added is not None:
                        pe.wait_ge(x_ready, added)
                    if needs is not None:
                        pe.wait_ge(*needs)
                    for a, kt in enumerate(kts):
                        wh, wl = (w[:, s, a * width:(a + 1) * width] for w in (w_hi, w_lo))
                        for m in range(MT):
                            rows = slice(m * P, (m + 1) * P)
                            last = three(acc[2 * acc_set + m][:, 0:width], src[0][:, kt, rows], src[1][:, kt, rows],
                                         wh, wl, start and a == 0, stop and a == len(kts) - 1)
                else:
                    pe.wait_ge(slo_ready, n.kt.value())
                    if start:
                        pe.wait_ge(acc_free[down], n.sets[down].value())
                        pe.wait_ge(hT_ready, n.hT.value())
                    for m in range(MT):
                        rows = slice(m * P, (m + 1) * P)
                        for b in range(2):
                            wh, wl = (w[:, s, b * NB:(b + 1) * NB] for w in (w_hi, w_lo))
                            last = three(down_bank[2 * down + b][m][:, :], stage_hi[:, stage, rows],
                                         stage_lo[:, stage, rows], wh, wl, start, stop)
                last.then_inc(half_used, 1)

            def four_by_two(src, banks, tiles=4):
                for t in range(tiles):
                    for m in range(MT):
                        at = (t % 2) * SEQ + m * P
                        last = pe.transpose(banks[t // 2][:, at:at + P], src(m, t), ident[:, :])
                return last

            def xT(gain, j, needs):
                n = e.n
                if needs is None:
                    pe.wait_ge(x_loaded[j], 32)
                else:
                    pe.wait_ge(x_ready, needs)
                if n.xT.c >= 2:
                    pe.wait_ge(xT_ready, n.xT.c - 1)
                if n.xT.c == 1:
                    pe.wait_ge(gains_ready, 1)
                four_by_two(lambda m, t: x[:, m, (4 * j + t) * P:(4 * j + t + 1) * P],
                            work[2 * (j % 2):2 * (j % 2) + 2]).then_inc(xT_done, 1)

            def qkT(src, dst, gain):
                n = e.n
                if gain is None or gain is False:
                    taken_out(pe, n)
                else:
                    pe.wait_ge(normed, n.norm.value())
                if n.head.past(1):
                    pe.wait_ge(o_ready, n.head.value())
                if n.oT.past(1):
                    pe.wait_ge(oT_ready, n.oT.value())
                banks = work[2:4] if dst is kT else work[0:2]
                four_by_two(lambda m, t: src[:, m, t * P:(t + 1) * P], banks,
                            2 if src is k_dup else 4).then_inc(qkT_done, 1)

            def oT(kt0):
                n = e.n
                pe.wait_ge(o_ready, n.head.value())
                pe.wait_ge(qkT_ready, n.qkT.value())
                four_by_two(lambda m, t: o_nat[:, m, t * P:(t + 1) * P], work[2:4]).then_inc(oT_done, 1)

            def hidden(j):
                n = e.n
                pe.wait_ge(acc_free[1], n.sets[1].value())
                if n.hT.past(1):
                    pe.wait_ge(hT_ready, n.hT.value())
                four_by_two(lambda m, t: hid[:, m, t * P:(t + 1) * P], work[2:4]).then_inc(hT_done, 1)

            def attend(what, h, kind, slope, kv):
                n, b = e.n, h % 2
                head = n.head.value(h + 1)
                rows = slice(b * HD, (b + 1) * HD)
                bank = work[h % 4]
                if what == "qk" and h == 0:
                    pe.wait_ge(qkT_ready, n.qkT.value())
                    taken_out(pe, n)
                if (what, kind) == ("qk", "soft"):
                    key = h // 2 if kv is None else kv
                    pe.matmul(work[b][:, 0:P], qT[rows, h // 2, 0:P], kT[rows, key, 0:P], start=True, stop=True)
                    pe.matmul(work[b][:, P:S384], qT[rows, h // 2, P:SEQ], kT[rows, key, :],
                              start=True, stop=True).then_inc(s_done, 1)
                if (what, kind) == ("mid", "soft"):
                    pe.wait_ge(mid_ready, head)
                    if h >= 2:
                        pe.wait_ge(o_ready, n.head.value(h - 1))
                    elif n.oT.past(1):
                        pe.wait_ge(oT_ready, n.oT.value())
                    for k in range(3):
                        last = pe.transpose(work[2 + b][:, k * P:(k + 1) * P], p_buf[:, b, k * P:(k + 1) * P],
                                            ident[:, :])
                    last.then_inc(mid_done, 1)
                if (what, kind) == ("qk", "stick"):
                    if h >= 4:
                        pe.wait_ge(o_ready, n.head.value(h - 3))
                    elif h >= 2:
                        pe.wait_ge(oT_ready, n.oT.value())
                    pe.matmul(bank[:, 0:SEQ], kT[rows, h // 2, 0:P], qT[rows, h // 2, :], start=True, stop=False,
                              skip_group_check=True)
                    pe.matmul(bank[:, SEQ:S384], kT[rows, h // 2, P:SEQ], qT[rows, h // 2, P:SEQ], start=False,
                              stop=False, skip_group_check=True).then_inc(s_done, 1)
                if (what, kind) == ("mid", "stick"):
                    pe.wait_ge(mid_ready, head)
                    pe.matmul(bank[:, 0:SEQ], c["tri"][:, :], t_buf[:, b, 0:SEQ], start=False, stop=False,
                              skip_group_check=True)
                    pe.matmul(bank[:, P:SEQ], c["ones"][:, :], t_buf[:, b, SEQ:S384], start=False, stop=False,
                              skip_group_check=True)
                    pe.matmul(bank[:, SEQ:S384], c["tri"][:, :], t_buf[:, b, SEQ:S384], start=False, stop=True,
                              skip_group_check=True).then_inc(mid_done, 1)
                if what == "pv":
                    pe.wait_ge(pt_ready, head)
                    pt, o = (t_buf, work[2 + b]) if kind == "soft" else (p_buf, bank)
                    vs = slice(h * HD, (h + 1) * HD) if kv is None else slice(kv * HD, (kv + 1) * HD)
                    pe.matmul(o[:, S384:S384 + HD], pt[:, b, 0:P], v_nat[:, 0, vs], start=True, stop=True)
                    pe.matmul(o[:, S384 + HD:NB], pt[:, b, P:SEQ], v_nat[:, 0, vs], start=True, stop=False)
                    pe.matmul(o[:, S384 + HD:NB], pt[:, b, SEQ:S384], v_nat[:, 1, vs], start=False,
                              stop=True).then_inc(o_done, 1)

            e = Steps(begin=begin, half=half, xT=xT, qkT=qkT, oT=oT, hidden=hidden, attend=attend)
            walk(pe, e)


_INS = ['x', 'attn_norm', 'ffn_norm', 'even_w_in', 'even_q_norm', 'even_k_norm', 'even_sinks', 'even_w_out',
        'odd_w_in', 'odd_q_norm', 'odd_k_norm', 'odd_w_out', 'ffn_w_gate', 'ffn_w_up', 'ffn_w_down']


def kernel(**inputs):
    import numpy as _np
    import concourse.bacc as _bacc
    from concourse import mybir as _mybir
    from concourse.bass_utils import run_bass_kernel_spmd as _run

    nc = _bacc.Bacc("TRN2", target_bir_lowering=False, num_devices=1)
    consts, widths, c_mask = make_constants(inputs['even_sinks'].shape[1], inputs['x'].shape[2] // HD)
    arrays, args = {}, []
    for name, a in [(name, inputs[name]) for name in _INS] + [('consts', consts), ('c_mask', c_mask)]:
        a = _np.ascontiguousarray(a)
        arrays[f"in_{name}_dram"] = a
        args.append(nc.dram_tensor(f"in_{name}_dram", a.shape, _mybir.dt.from_np(a.dtype), kind="ExternalInput").ap())
    args.append(nc.dram_tensor("out_0_dram", inputs['x'].shape, _mybir.dt.float32, kind="ExternalOutput").ap())
    decoder_kernel(nc, widths, *args)
    r = _run(nc, [arrays], core_ids=[0])
    return r.results[0]["out_0_dram"]
```

```python
from contextlib import ExitStack, contextmanager

import numpy as np

import concourse.bass as bass
from concourse import mybir

F32 = mybir.dt.float32
F32R = mybir.dt.float32r
ALU = mybir.AluOpType
ACT = mybir.ActivationFunctionType
AX_X = mybir.AxisListType.X

P = 128
HD = 64
GROUP = 8
NB = 512
CHUNK = 4 * NB
HALF = CHUNK // 2
RAW = 4
SPLIT = 4
AHEAD = 3
EPS = 1e-6
NEG = -1e30
S384 = 3 * P

SLOTS24 = ([1, 3, 5, 7, 10, 12, 15, 17], 2, 4)
SLOTS18 = ([0, 2, 4, 6, 8, 10, 12, 13], 2, 4)
SLOTS16 = ([0, 2, 4, 5, 7, 9, 11, 12], 2, 3)


class Count:

    def __init__(self):
        self.c, self.per, self.i = 0, 0, None

    def past(self, n):
        return self.i is not None or self.c >= n

    def value(self, more=0, unit=1):
        at = (self.c + more) * unit
        return at if self.i is None else self.i * (self.per * unit) + at

    def slot(self, ring, more=0):
        assert self.per % ring == 0
        return (self.c + more) % ring

    def turn(self, ring, more=0, plus=0, unit=1):
        at = ((self.c + more) // ring + plus) * unit
        return at if self.i is None else self.i * (self.per // ring * unit) + at


class Counts:

    def __init__(self):
        self.half = Count()
        self.chunk = Count()
        self.x = Count()
        self.xT = Count()
        self.rms = Count()
        self.norm = Count()
        self.qkT = Count()
        self.head = Count()
        self.oT = Count()
        self.hT = Count()
        self.kt = Count()
        self.sets = [Count(), Count()]

    @contextmanager
    def loop(self, eng, rounds, sets=(0, 0), **per):
        known = {"half": self.half, "chunk": self.chunk, "norm": self.norm, "qkT": self.qkT, "head": self.head,
                 "oT": self.oT, "hT": self.hT, "kt": self.kt}
        every = [(v, per.get(k, 0)) for k, v in known.items()] + list(zip(self.sets, sets))
        start = [v.c for v, _ in every]
        with eng.Fori(0, rounds) as i:
            for v, k in every:
                v.i, v.per = (i, k) if k else (None, 0)
            yield i
            for (v, k), c in zip(every, start):
                assert v.c == c + k, (v.c, c, k)
                v.i, v.c, v.per = None, c + rounds * k, 0


def steps_at(slots, k):
    qk, mid, last = slots
    out = []
    for h in range(GROUP):
        if qk[h] + last == k:
            out.append(("pv", h))
    for h in range(GROUP):
        if qk[h] + mid == k:
            out.append(("mid", h))
    for h in range(GROUP):
        if qk[h] == k:
            out.append(("qk", h))
    return out


def make_constants(n_a, n_c):
    q = np.arange(P)[:, None]
    k = np.arange(P)[None, :]
    dist = np.concatenate([q - k, q + P - k, q - k], 1)
    in_a = (dist >= 0) & (dist < 128)
    count = (((dist >= 0) & (dist <= 128)).astype(int) + ((dist >= 0) & (dist % 4 == 0))
             + ((dist >= 0) & (dist % 16 == 0)))
    c_mask = np.where(count > 0, np.log(np.maximum(count, 1)), NEG)
    keep = np.concatenate([k > q, np.ones((P, P)), k > q], 1)
    parts = {
        "minus_dist": -np.maximum(dist, 0.0),
        "a_mask": np.where(in_a, 0.0, NEG),
        "b_keep": keep,
        "b_mask": np.where(keep > 0, 0.0, NEG),
        "ident": np.eye(P),
        "tri": np.where(q >= k, -1.0, 0.0),
        "ones": np.full((P, P), -1.0),
        "slopes": np.tile(np.concatenate([2.0 ** (-8.0 * np.arange(1, n_a + 1) / n_a),
                                          2.0 ** (-8.0 * np.arange(1, n_c + 1) / n_c)]), (P, 1)),
        "half": np.full((P, 16), -0.5),
    }
    return np.concatenate([v.astype(np.float32) for v in parts.values()], 1), \
        {n: v.shape[1] for n, v in parts.items()}, c_mask.astype(np.float32)


def decoder_kernel(nc, widths, x_in, attn_norm, ffn_norm, even_w_in, even_q_norm, even_k_norm, even_sinks,
                   even_w_out, odd_w_in, odd_q_norm, odd_k_norm, odd_w_out, w_gate, w_up, w_down,
                   consts, c_mask_in, out):
    _, SEQ, D = x_in.shape
    FF = w_gate.shape[2]
    MT = SEQ // P
    KT = D // P
    JB = D // NB
    FB = FF // NB
    FK = FF // P
    NA = even_sinks.shape[1]
    NC = D // HD
    CG = NC // GROUP
    assert MT == 2 and KT == 16 and JB == 4 and NA == 2 * GROUP and FF % NB == 0
    AQ, AK = NA * HD, 2 * HD
    OFF, at = {}, 0
    for name, width in widths.items():
        OFF[name] = at
        at += width
    BIG = ("minus_dist", "a_mask", "b_keep", "b_mask", "tri", "ones")
    CONSTS = len(widths) - 1 - len(BIG) + 8 + 1
    HALVES = 4 + 8 * 8 + 2 * 4 * 8 + 3 * CG * 8 + 2 * (2 * FB * 8 + FK * 2)
    BQ = AQ + 2 * AK

    with ExitStack() as ctx:
        def sb(name, shape, dt, stack=ctx):
            return stack.enter_context(nc.sbuf_tensor(name, shape, dt))

        def sem(name):
            return ctx.enter_context(nc.semaphore(name))

        raw = sb("raw", [P, RAW, CHUNK], F32)
        w_hi = sb("w_hi", [P, SPLIT, HALF], F32R)
        w_lo = sb("w_lo", [P, SPLIT, HALF], F32R)
        x = sb("x", [P, MT, D], F32)
        xT_hi = sb("xT_hi", [P, KT, SEQ], F32R)
        xT_lo = sb("xT_lo", [P, KT, SEQ], F32R)
        s_buf = sb("s_buf", [P, 2, S384], F32)
        p_buf = sb("p_buf", [P, 2, S384], F32)
        t_buf = sb("t_buf", [P, 2, S384], F32)
        c = {n: sb(n, [P, w], F32) for n, w in widths.items()}
        ident = c["ident"]
        gains = sb("gains", [P, 2 * 2 * KT], F32)
        qk_gain = sb("qk_gain", [P, 4], F32)
        sinks = sb("sinks", [P, NA], F32)
        sumsq = sb("sumsq", [P, MT, JB], F32)
        msq = sb("msq", [P, MT], F32)
        rstd = sb("rstd", [P, MT], F32)
        hsum = sb("hsum", [P, MT * GROUP], F32)
        hrstd = sb("hrstd", [P, MT * GROUP], F32)
        smax = sb("smax", [P, 2, 2], F32)
        nmax = sb("nmax", [P, 2, 2], F32)
        den = sb("den", [P, 2, 2], F32)
        sink_e = sb("sink_e", [P, 2, 2], F32)
        rden = sb("rden", [P, 2, 2], F32)
        with ExitStack() as s1:
            hT = sb("hT", [P, FK, SEQ], F32, s1)
            stage_hi = sb("stage_hi", [P, 4, SEQ], F32R, s1)
            stage_lo = sb("stage_lo", [P, 4, SEQ], F32R, s1)
            silu_g = sb("silu_g", [P, MT, NB], F32, s1)
            hid = sb("hid", [P, MT, NB], F32, s1)
        oT_hi = sb("oT_hi", [P, KT, SEQ], F32R)
        oT_lo = sb("oT_lo", [P, KT, SEQ], F32R)
        q_nat = sb("q_nat", [P, MT, NB], F32)
        k_nat = sb("k_nat", [P, MT, NB], F32)
        v_nat = sb("v_nat", [P, MT, NB], F32)
        qT = sb("qT", [P, 4, SEQ], F32)
        kT = sb("kT", [P, 4, SEQ], F32)
        sq = sb("sq", [P, MT, NB], F32)
        o_nat = sb("o_nat", [P, MT, NB], F32)

        acc = [ctx.enter_context(nc.psum_tensor(f"acc{i}", [P, NB], F32)) for i in range(4)]
        work = [ctx.enter_context(nc.psum_tensor(f"work{i}", [P, NB], F32)) for i in range(4)]
        down_bank = [work[0:2], acc[0:2], work[2:4], acc[2:4]]

        raw_loaded = [sem(f"raw_loaded{i}") for i in range(RAW)]
        const_loaded = sem("const_loaded")
        big_loaded = sem("big_loaded")
        x_loaded = [sem(f"x_loaded{j}") for j in range(JB)]
        gain_loaded = sem("gain_loaded")
        mask_loaded = sem("mask_loaded")
        hi_ready = sem("hi_ready")
        lo_ready = sem("lo_ready")
        half_used = sem("half_used")
        acc_free = [sem(f"acc_free{i}") for i in range(2)]
        gainT_done = sem("gainT_done")
        gains_ready = sem("gains_ready")
        x_ready = sem("x_ready")
        xT_done = sem("xT_done")
        xhi_ready = sem("xhi_ready")
        xT_ready = sem("xT_ready")
        sumsq_ready = sem("sumsq_ready")
        msq_ready = sem("msq_ready")
        rstd_ready = sem("rstd_ready")
        hsum_ready = sem("hsum_ready")
        hrstd_ready = sem("hrstd_ready")
        normed = sem("normed")
        qkT_done = sem("qkT_done")
        qkT_ready = sem("qkT_ready")
        s_done = sem("s_done")
        s_ready = sem("s_ready")
        mid_done = sem("mid_done")
        pt_ready = sem("pt_ready")
        log_ready = sem("log_ready")
        mid_ready = sem("mid_ready")
        o_done = sem("o_done")
        o_ready = sem("o_ready")
        oT_done = sem("oT_done")
        ohi_ready = sem("ohi_ready")
        oT_ready = sem("oT_ready")
        hT_done = sem("hT_done")
        hT_ready = sem("hT_ready")
        shi_ready = sem("shi_ready")
        slo_ready = sem("slo_ready")
        abs_ready = sem("abs_ready")
        exp_ready = sem("exp_ready")
        sum_made = sem("sum_made")
        sq_made = sem("sq_made")
        hsum_made = sem("hsum_made")
        dist_added = sem("dist_added")
        max_made = sem("max_made")
        den_made = sem("den_made")
        rden_made = sem("rden_made")
        sp_made = sem("sp_made")
        qgain_made = sem("qgain_made")
        stored = sem("stored")

        def heads_view(t):
            return t.rearrange("p m (h d) -> p (m h) d", d=HD)

        k_dup = k_nat[:, 0, :].rearrange("p (m n) -> p m n", m=MT)

        def taken_out(eng, n):
            eng.wait_ge(acc_free[0], n.sets[0].value())
            if n.sets[1].past(1):
                eng.wait_ge(acc_free[1], n.sets[1].value())

        def walk(eng, e):
            n = Counts()
            e.n = n

            def half(**what):
                e.half(**what)
                n.half.c += 1

            def evacuate(dst, acc_set, scaled=True):
                e.evacuate(dst, acc_set)
                n.sets[acc_set].c += 1

            def xT(gain, j, needs=None):
                e.xT(gain, j, needs)
                n.xT.c += 1

            def norm_a(t):
                e.norm_a(t)

            def norm_b(t):
                e.norm_b(t)
                n.norm.c += 1

            def qkT(src, dst, gain):
                e.qkT(src, dst, gain)
                n.qkT.c += 1

            def oT(kt0, later=0):
                e.oT(kt0, later)
                n.oT.c += 1

            def attend(slots, k, kind, layer_c=None, kv=None):
                for what, h in steps_at(slots, k):
                    e.attend(what, h, kind, layer_c, kv)
                if k == slots[0][-1] + slots[2]:
                    n.head.c += GROUP

            def block(acc_set, src=(xT_hi, xT_lo), extra=None, first=False, added=None):
                x0 = n.xT.c // JB * JB if n.xT.c % JB else n.xT.c - JB
                for k in range(8):
                    half(src=src, kts=(2 * k, 2 * k + 1), acc_set=acc_set, start=k == 0, stop=k == 7,
                         needs=(xT_ready, x0 + k // 2 + 1) if first else None, added=added)
                    if extra:
                        extra(k)

            def residual(banks, halves_behind=0):
                e.residual(banks, halves_behind)
                n.x.c += 1

            def rms():
                for j in range(JB):
                    e.squares(j)
                e.rms()
                n.rms.c += 1

            def out_projection(gain, kind, layer_c, first_oT=None):
                src = (oT_hi, oT_lo)
                o0 = n.oT.c // CG * CG
                last = KT // 2 - 2
                k = 0
                for j in range(JB):
                    for cc in range(last):
                        half(src=src, kts=(2 * cc, 2 * cc + 1), acc_set=j % 2, start=cc == 0, stop=cc == last - 1,
                             needs=(oT_ready, o0 + cc // 2 + 1))
                        attend(SLOTS24, k, kind, layer_c)
                        if k == 1 and first_oT is not None:
                            oT(first_oT)
                        if k == 22:
                            oT(3 * 4)
                        k += 1
                    e.partial(acc[2 * (j % 2):2 * (j % 2) + 2], j)
                    n.sets[j % 2].c += 1
                x0 = n.x.c
                for j in range(JB):
                    for cc in (last, last + 1):
                        half(src=src, kts=(2 * cc, 2 * cc + 1), acc_set=j % 2, start=cc == last,
                             stop=cc == last + 1, needs=(oT_ready, o0 + 4), added=x0 + j - 1 if j >= 2 else None)
                    residual(acc[2 * (j % 2):2 * (j % 2) + 2])
                    if j >= 1:
                        xT(gain, j - 1, x0 + j)

            def feed_forward(layer):
                x0 = n.x.c
                block(0, extra=lambda k: xT(2 + layer, 3, x0) if k == 1 else rms() if k == 3 else None, first=True,
                      added=x0 - 1)
                e.gate(0)
                n.sets[0].c += 1
                block(1, added=x0)
                e.up(1)
                n.sets[1].c += 1

                def hidden(j):
                    e.hidden(j)
                    n.hT.c += 1

                with n.loop(eng, FB - 1, half=16, sets=(1, 1), hT=1) as j:
                    block(0, extra=lambda k: hidden(j) if k == 2 else None)
                    e.gate(0)
                    n.sets[0].c += 1
                    block(1)
                    e.up(1)
                    n.sets[1].c += 1

                def stage(kt, slot):
                    e.stage(kt, slot)
                    n.kt.c += 1

                def four(at, start=False, stop=False):
                    for t in range(4):
                        half(down=0, stage=t, start=start and t == 0, stop=stop and t == 3)
                        if start and t == 0:
                            hidden(FB - 1)
                        if not (stop and t == 3):
                            stage(at + t + 1, (t + 1) % 4)
                        half(down=1, stage=t, start=start and t == 0, stop=stop and t == 3)

                stage(0, 0)
                four(0, start=True)
                with n.loop(eng, FK // 4 - 2, half=8, kt=4) as j:
                    four(j * 4 + 4)
                four(FK - 4, stop=True)

            e.begin()
            xT(0, 0)
            xT(0, 1)
            e.first_splits()
            for k in range(4):
                if 0 < k < 3:
                    xT(0, k + 1)
                half(src=(xT_hi, xT_lo), kts=range(4 * k, 4 * k + 4), acc_set=0, start=k == 0, stop=k == 3,
                     width=2 * P, needs=(xT_ready, k + 1))
            rms()
            e.evacuate_kv()
            n.sets[0].c += 1
            block(1, extra=lambda k: norm_a(k_dup) if k == 1 else norm_b(k_dup) if k == 3 else None)
            evacuate(q_nat, 1)

            def layer0(t):
                if t == 0:
                    norm_a(q_nat)
                if t == 2:
                    norm_b(q_nat)
                if t == 3:
                    qkT(k_dup, kT, 1)
                    qkT(q_nat, qT, 0)
                if 4 <= t < 20:
                    attend(SLOTS16, t - 4, "soft", 0, 0)
                if t == 9:
                    norm_a(q_nat)
                if t == 11:
                    norm_b(q_nat)
                if t == 20:
                    qkT(q_nat, qT, 0)
                    evacuate(q_nat, 1)
                    oT(0, later=2)
                if 21 <= t < 37:
                    attend(SLOTS16, t - 21, "soft", GROUP, 1)
                if t == 36:
                    evacuate(v_nat, 1)
                if t == 37:
                    qkT(q_nat, qT, None)
                    qkT(k_nat, kT, False)
                if t >= 38:
                    attend(SLOTS18, t - 38, "stick")
                if t == 38:
                    oT(4)

            block(0, extra=layer0)
            evacuate(q_nat, 0)
            block(1, extra=lambda k: layer0(8 + k))
            block(0, extra=lambda k: layer0(16 + k))
            evacuate(k_nat, 0)
            block(1, extra=lambda k: layer0(24 + k))
            block(0, extra=lambda k: layer0(32 + k))
            evacuate(q_nat, 0)
            block(1, extra=lambda k: layer0(40 + k))
            evacuate(k_nat, 1)
            block(0, extra=lambda k: layer0(48 + k))
            evacuate(v_nat, 0)
            qkT(q_nat, qT, None)
            qkT(k_nat, kT, False)
            out_projection(2, "stick", None, first_oT=8)
            feed_forward(0)

            def after_down(gain):
                x0 = n.x.c
                residual(down_bank[0], 1)
                residual(down_bank[1], 1)
                residual(down_bank[2])
                xT(gain, 0, x0 + 1)
                residual(down_bank[3])
                xT(gain, 1, x0 + 3)
                return lambda k: (xT(gain, 2, x0 + 4) if k == 1 else xT(gain, 3, x0 + 4) if k == 3 else
                                  rms() if k == 4 else None)

            block(0, extra=after_down(1), first=True)
            evacuate(q_nat, 0)
            block(1, extra=lambda k: norm_a(q_nat) if k == 1 else norm_b(q_nat) if k == 3 else None)
            evacuate(k_nat, 1)
            block(0, extra=lambda k: norm_a(k_nat) if k == 1 else norm_b(k_nat) if k == 3 else None)
            evacuate(v_nat, 0)
            qkT(q_nat, qT, 2)
            qkT(k_nat, kT, 3)
            with n.loop(eng, CG - 1, half=24, norm=2, qkT=2, head=GROUP, oT=1, sets=(2, 1)) as g:
                slope0 = g * GROUP + NA
                block(0, extra=lambda k: attend(SLOTS24, k, "soft", slope0))
                evacuate(q_nat, 0)

                def c2(k):
                    attend(SLOTS24, k + 8, "soft", slope0)
                    if k == 1:
                        norm_a(q_nat)
                    if k == 3:
                        norm_b(q_nat)
                block(1, extra=c2)
                evacuate(k_nat, 1)

                def c3(k):
                    attend(SLOTS24, k + 16, "soft", slope0)
                    if k == 1:
                        norm_a(k_nat)
                    if k == 3:
                        norm_b(k_nat)
                    if k == 6:
                        qkT(q_nat, qT, 2)
                        oT(g * 4, later=1)
                block(0, extra=c3)
                evacuate(v_nat, 0)
                qkT(k_nat, kT, 3)
            out_projection(3, "soft", NA + (CG - 1) * GROUP)
            feed_forward(1)
            for j in range(JB):
                residual(down_bank[j], 1 if j < 2 else 0)

        def nothing(*args, **named):
            return None

        class Steps:

            def __init__(self, begin=nothing, first_splits=nothing, half=nothing, evacuate=nothing, evacuate_kv=nothing, xT=nothing,
                         norm_a=nothing, norm_b=nothing, qkT=nothing, oT=nothing, attend=nothing, residual=nothing,
                         partial=nothing,
                         squares=nothing, rms=nothing, gate=nothing, up=nothing, hidden=nothing, stage=nothing):
                self.n, self.first_splits, self.partial = None, first_splits, partial
                self.begin, self.half, self.evacuate, self.evacuate_kv = begin, half, evacuate, evacuate_kv
                self.xT, self.norm_a, self.norm_b, self.qkT, self.oT = xT, norm_a, norm_b, qkT, oT
                self.attend, self.residual, self.squares, self.rms = attend, residual, squares, rms
                self.gate, self.up, self.hidden, self.stage = gate, up, hidden, stage

        block = ctx.enter_context(nc.Block())

        @block.sync
        def _(sp):
            n = Counts()

            def chunk(src, tiles=None):
                if n.chunk.past(RAW):
                    sp.wait_ge(lo_ready, n.chunk.value(1 - RAW, unit=2))
                s = n.chunk.slot(RAW)
                dst = raw[:, s, :]
                if tiles:
                    dst = dst.rearrange("p (t n) -> p t n", t=tiles)
                sp.dma_start(dst, src).then_inc(raw_loaded[s], 16)
                n.chunk.c += 1

            def columns(w, cols, which=range(KT // 4)):
                wv = w.rearrange("(c t p) n -> c p t n", t=4, p=P)
                for k in which:
                    chunk(wv[k][:, :, cols], 4)

            def out_projection(w):
                for which in (range(3), [3]):
                    for j in range(JB):
                        columns(w, slice(j * NB, (j + 1) * NB), which)

            def feed_forward(layer):
                with n.loop(sp, FB, chunk=8) as j:
                    columns(w_gate[layer], bass.ds(j * NB, NB))
                    columns(w_up[layer], bass.ds(j * NB, NB))
                with n.loop(sp, FK // 4, chunk=4) as j:
                    for t in range(4):
                        chunk(w_down[layer][bass.ds(j * (4 * P) + t * P, P), :])

            kv = even_w_in[0].rearrange("(c t p) n -> c p t n", t=8, p=P)
            for j in range(JB):
                for m in range(MT):
                    sp.dma_start(x[:, m, j * NB:(j + 1) * NB],
                                 x_in[0, m * P:(m + 1) * P, j * NB:(j + 1) * NB]).then_inc(x_loaded[j], 16)
                if j in (0, JB - 1):
                    chunk(kv[j // 2][:, :, AQ:AQ + 2 * AK], 8)
            columns(even_w_in[0], slice(0, NB), range(2))
            for name in BIG:
                sp.dma_start(c[name][:, :], consts[:, OFF[name]:OFF[name] + widths[name]]).then_inc(big_loaded, 16)
            columns(even_w_in[0], slice(0, NB), range(2, KT // 4))
            for first in [NB] + [BQ + t * AQ + g * NB for g in range(2) for t in range(3)]:
                columns(even_w_in[0], slice(first, first + NB))
            out_projection(even_w_out[0])
            feed_forward(0)
            sp.wait_ge(s_ready, 2 * GROUP)
            sp.dma_start(c["a_mask"][:, :], c_mask_in).then_inc(mask_loaded, 16)
            with n.loop(sp, CG, chunk=12) as g:
                for t in range(3):
                    columns(odd_w_in[0], bass.ds(g * NB + t * D, NB))
            out_projection(odd_w_out[0])
            feed_forward(1)
            for j in range(JB):
                sp.wait_ge(x_ready, 3 * JB + j + 1)
                for m in range(MT):
                    sp.dma_start(out[0, m * P:(m + 1) * P, j * NB:(j + 1) * NB],
                                 x[:, m, j * NB:(j + 1) * NB]).then_inc(stored, 16)
            sp.wait_ge(stored, 16 * JB * MT)

        @block.gpsimd
        def _(pool):
            def begin():
                for name in widths:
                    if name not in BIG and name != "ident":
                        pool.dma_start(c[name][:, :],
                                       consts[:, OFF[name]:OFF[name] + widths[name]]).then_inc(const_loaded, 16)
                for col, g in enumerate((even_q_norm, even_k_norm, odd_q_norm, odd_k_norm)):
                    for r in range(2):
                        pool.dma_start(qk_gain[r * HD:(r + 1) * HD, col:col + 1],
                                       g.rearrange("a d -> d a")).then_inc(const_loaded, 16)
                pool.dma_start(sinks[:, :], even_sinks[0:1, :].broadcast_to([P, NA])).then_inc(const_loaded, 16)
                pool.wait_ge(const_loaded, 16 * CONSTS)

            def rms():
                pool.wait_ge(msq_ready, e.n.rms.value(1))
                pool.tensor_tensor(rstd[:, :], msq[:, :], c["half"][:, 0:MT], ALU.pow).then_inc(rstd_ready, 1)

            def norm_b(t):
                pool.wait_ge(hsum_ready, e.n.norm.value(1))
                w = GROUP if t is k_dup else MT * GROUP
                pool.tensor_tensor(hrstd[:, 0:w], hsum[:, 0:w], c["half"][:, 0:w], ALU.pow).then_inc(hrstd_ready, 1)

            e = Steps(begin=begin, rms=rms, norm_b=norm_b)
            walk(pool, e)

        @block.scalar
        def _(act):
            def split(more):
                n = e.n
                if n.half.i is None and n.half.c + more >= HALVES:
                    return
                s, r = n.half.slot(SPLIT, more), n.half.slot(2 * RAW, more)
                act.wait_ge(raw_loaded[r // 2], n.half.turn(2 * RAW, more, plus=1, unit=16))
                if n.half.i is not None or n.half.c + more >= SPLIT:
                    act.wait_ge(half_used, n.half.value(more + 1 - SPLIT))
                act.activation(w_hi[:, s, :], raw[:, r // 2, (r % 2) * HALF:(r % 2 + 1) * HALF],
                               ACT.Copy).then_inc(hi_ready, 1)

            def begin():
                act.dma_start(ident[:, :], consts[:, OFF["ident"]:OFF["ident"] + P]).then_inc(gain_loaded, 16)
                for r, g in ((0, attn_norm), (2 * KT, ffn_norm)):
                    act.dma_start(s_buf[r:r + 2 * KT, 0, 0:P],
                                  g.rearrange("l (t p) -> (l t) p", p=P)).then_inc(gain_loaded, 16)
                act.wait_ge(gainT_done, 1)
                act.activation(gains[:, :], work[3][:, 0:4 * KT], ACT.Copy).then_inc(gains_ready, 1)
                act.wait_ge(gains_ready, 1)

            def first_splits():
                for k in range(AHEAD):
                    split(k)

            def evacuate(dst, acc_set):
                n = e.n
                act.wait_ge(half_used, n.half.value())
                act.wait_ge(rstd_ready, n.rms.value())
                if dst is v_nat:
                    act.wait_ge(o_done, n.head.value())
                elif n.qkT.past(1):
                    act.wait_ge(qkT_done, n.qkT.value())
                for m in range(MT):
                    last = act.activation(dst[:, m, :], acc[2 * acc_set + m][:, :], ACT.Copy, scale=rstd[:, m:m + 1])
                last.then_inc(acc_free[acc_set], 1)

            def evacuate_kv():
                act.wait_ge(half_used, e.n.half.value())
                act.wait_ge(rstd_ready, 1)
                for m in range(MT):
                    for g in range(2):
                        for r in range(2):
                            act.activation(k_dup[:, m, (2 * g + r) * HD:(2 * g + r + 1) * HD],
                                           acc[m][:, g * HD:(g + 1) * HD], ACT.Copy, scale=rstd[:, m:m + 1])
                    last = act.activation(v_nat[:, m, 0:AK], acc[m][:, AK:2 * AK], ACT.Copy, scale=rstd[:, m:m + 1])
                last.then_inc(acc_free[0], 1)

            def xT_high(gain, j, needs):
                act.wait_ge(xT_done, e.n.xT.value(1))
                for t in range(4):
                    kt = 4 * j + t
                    last = act.activation(xT_hi[:, kt, :],
                                          work[2 * (j % 2) + t // 2][:, (t % 2) * SEQ:(t % 2 + 1) * SEQ],
                                          ACT.Copy, scale=gains[:, gain * KT + kt:gain * KT + kt + 1])
                last.then_inc(xhi_ready, 1)

            def squares(j):
                n = e.n
                if n.rms.c == 0:
                    act.wait_ge(x_loaded[j], 32)
                else:
                    act.wait_ge(x_ready, n.x.c - JB + j + 1)
                if n.rms.c or j:
                    act.wait_ge(sumsq_ready, n.rms.c * JB + j)
                for m in range(MT):
                    waste = (t_buf, p_buf)[m][:, :, :].rearrange("p a b -> p (a b)")[:, 0:NB]
                    last = act.activation(waste, x[:, m, j * NB:(j + 1) * NB], ACT.Square,
                                          accum_out=sumsq[:, m, j:j + 1])
                last.then_inc(sumsq_ready, 1)

            def qkT(src, dst, gain):
                act.wait_ge(qkT_done, e.n.qkT.value(1))
                if e.n.qkT.c == 0 and e.n.qkT.i is None:
                    act.wait_ge(qgain_made, 1)
                banks = work[2:4] if dst is kT else work[0:2]
                if src is k_dup:
                    banks = banks[0:1]
                scale = qk_gain[:, gain:gain + 1] if gain is not None and gain is not False else (
                    HD ** -0.5 if gain is None else 1.0)
                for b, bank in enumerate(banks):
                    last = act.activation(dst[:, 2 * b:2 * b + 2, :].rearrange("p a b -> p (a b)"), bank[:, :],
                                          ACT.Copy, scale=scale)
                last.then_inc(qkT_ready, 1)

            def oT(kt0, later):
                act.wait_ge(oT_done, e.n.oT.value(1))
                for b in range(2):
                    last = act.activation(oT_hi[:, bass.ds(kt0 + 2 * b, 2), :].rearrange("p a b -> p (a b)"),
                                          work[2 + b][:, :], ACT.Copy)
                last.then_inc(ohi_ready, 1)

            def attend(what, h, kind, slope, kv):
                n, b = e.n, h % 2
                head = n.head.value(h + 1)
                if (what, kind) == ("qk", "soft"):
                    act.wait_ge(s_ready, head)
                    for m, (lo, hi) in enumerate(((0, P), (P, S384))):
                        last = act.activation(p_buf[:, b, lo:hi], s_buf[:, b, lo:hi], ACT.Exp,
                                              bias=nmax[:, b, m:m + 1], accum_out=den[:, b, m:m + 1])
                    if kv is not None:
                        last = act.activation(sink_e[:, b, :], nmax[:, b, :], ACT.Exp,
                                              bias=sinks[:, slope + h:slope + h + 1])
                    last.then_inc(mid_ready, 1)
                if (what, kind) == ("mid", "soft"):
                    act.wait_ge(mid_done, head)
                    if n.head.past(2) or h >= 2:
                        act.wait_ge(o_done, n.head.value(h - 1))
                    act.activation(t_buf[:, b, :], work[2 + b][:, 0:S384], ACT.Copy).then_inc(pt_ready, 1)
                if (what, kind) == ("qk", "stick"):
                    act.wait_ge(s_done, head)
                    k = head - NA
                    act.activation(s_buf[:, b, :], work[h % 4][:, 0:S384], ACT.Abs).then_inc(abs_ready, 1)
                    act.wait_ge(abs_ready, k)
                    act.activation(s_buf[:, b, :], s_buf[:, b, :], ACT.Exp, scale=-1.0).then_inc(exp_ready, 1)
                    act.wait_ge(exp_ready, k)
                    act.activation(s_buf[:, b, :], s_buf[:, b, :], ACT.Ln, bias=1.0).then_inc(log_ready, 1)
                if (what, kind) == ("mid", "stick"):
                    act.wait_ge(s_ready, head)
                    act.wait_ge(o_done, n.head.value(h - 1))
                    act.activation(p_buf[:, b, :], s_buf[:, b, :], ACT.Exp).then_inc(pt_ready, 1)

            def gate(acc_set):
                n = e.n
                act.wait_ge(half_used, n.half.value())
                act.wait_ge(rstd_ready, n.rms.value())
                if n.sets[1].past(1):
                    act.wait_ge(acc_free[1], n.sets[1].value())
                for m in range(MT):
                    last = act.activation(silu_g[:, m, :], acc[2 * acc_set + m][:, :], ACT.Silu,
                                          scale=rstd[:, m:m + 1])
                last.then_inc(acc_free[acc_set], 1)

            def hidden(j):
                act.wait_ge(hT_done, e.n.hT.value(1))
                for b in range(2):
                    last = act.activation(hT[:, bass.ds(j * 4 + 2 * b, 2), :].rearrange("p a b -> p (a b)"),
                                          work[2 + b][:, :], ACT.Copy)
                last.then_inc(hT_ready, 1)

            def stage(kt, t):
                n = e.n
                act.wait_ge(hT_ready, n.hT.value())
                if n.kt.past(4):
                    act.wait_ge(half_used, n.half.value(-5))
                act.activation(stage_hi[:, t, :], hT[:, bass.ds(kt, 1), :].rearrange("p a b -> p (a b)"),
                               ACT.Copy).then_inc(shi_ready, 1)

            e = Steps(begin=begin, first_splits=first_splits, half=lambda **w: split(AHEAD), evacuate=evacuate, evacuate_kv=evacuate_kv,
                      xT=xT_high, squares=squares, qkT=qkT, oT=oT, attend=attend, gate=gate, hidden=hidden,
                      stage=stage)
            walk(act, e)

        @block.vector
        def _(dve):
            def split(more):
                n = e.n
                if n.half.i is None and n.half.c + more >= HALVES:
                    return
                s, r = n.half.slot(SPLIT, more), n.half.slot(2 * RAW, more)
                dve.wait_ge(hi_ready, n.half.value(more + 1))
                dve.tensor_tensor(w_lo[:, s, :], raw[:, r // 2, (r % 2) * HALF:(r % 2 + 1) * HALF],
                                  w_hi[:, s, :].bitcast(F32), ALU.subtract).then_inc(lo_ready, 1)

            def first_splits():
                for k in range(AHEAD - 1):
                    split(k)

            def evacuate_kv():
                dve.wait_ge(const_loaded, 16 * CONSTS)
                for col in (0, 2):
                    last = dve.tensor_scalar(qk_gain[:, col:col + 1], qk_gain[:, col:col + 1], HD ** -0.5, None,
                                             ALU.mult)
                last.then_inc(qgain_made, 1)

            def xT_low(gain, j, needs):
                dve.wait_ge(xhi_ready, e.n.xT.value(1))
                for t in range(4):
                    kt = 4 * j + t
                    last = dve.scalar_tensor_tensor(
                        out=xT_lo[:, kt, :], in0=work[2 * (j % 2) + t // 2][:, (t % 2) * SEQ:(t % 2 + 1) * SEQ],
                        scalar=gains[:, gain * KT + kt:gain * KT + kt + 1], in1=xT_hi[:, kt, :].bitcast(F32),
                        op0=ALU.mult, op1=ALU.subtract)
                last.then_inc(xT_ready, 1)

            def rms():
                k = e.n.rms.value(1)
                dve.wait_ge(sumsq_ready, k * JB)
                dve.tensor_reduce(msq[:, :], sumsq[:, :, :], AX_X, ALU.add).then_inc(sum_made, 1)
                dve.wait_ge(sum_made, k)
                dve.tensor_scalar(msq[:, :], msq[:, :], 1.0 / D, EPS, ALU.mult, ALU.add).then_inc(msq_ready, 1)

            def norm_a(t):
                k = e.n.norm.value(1)
                v = heads_view(t)
                w = v.shape[1]
                sqv = sq[:, :, :].rearrange("p m n -> p (m n)")[:, 0:w * HD].rearrange("p (h d) -> p h d", d=HD)
                taken_out(dve, e.n)
                dve.tensor_tensor(sqv, v, v, ALU.mult).then_inc(sq_made, 1)
                dve.wait_ge(sq_made, k)
                dve.tensor_reduce(hsum[:, 0:w], sqv, AX_X, ALU.add).then_inc(hsum_made, 1)
                dve.wait_ge(hsum_made, k)
                dve.tensor_scalar(hsum[:, 0:w], hsum[:, 0:w], 1.0 / HD, EPS, ALU.mult, ALU.add).then_inc(hsum_ready, 1)

            def norm_b(t):
                v = heads_view(t)
                w = v.shape[1]
                dve.wait_ge(hrstd_ready, e.n.norm.value(1))
                dve.tensor_tensor(v, v, hrstd[:, 0:w].unsqueeze(2).broadcast_to([P, w, HD]),
                                  ALU.mult).then_inc(normed, 1)

            def oT(kt0, later):
                dve.wait_ge(ohi_ready, e.n.oT.value(1))
                for b in range(2):
                    at = bass.ds(kt0 + 2 * b, 2)
                    last = dve.tensor_tensor(oT_lo[:, at, :].rearrange("p a b -> p (a b)"), work[2 + b][:, :],
                                             oT_hi[:, at, :].rearrange("p a b -> p (a b)").bitcast(F32), ALU.subtract)
                last.then_inc(oT_ready, 1)

            def attend(what, h, kind, slope, kv):
                n, b = e.n, h % 2
                head = n.head.value(h + 1)
                if (what, kind) == ("qk", "soft"):
                    at = bass.ds(slope + h, 1)
                    if kv == 0 and h == 0:
                        dve.wait_ge(big_loaded, 16 * len(BIG))
                    dve.wait_ge(s_done, head)
                    dve.scalar_tensor_tensor(out=s_buf[:, b, :], in0=c["minus_dist"][:, :], scalar=c["slopes"][:, at],
                                             in1=work[b][:, 0:S384], op0=ALU.mult, op1=ALU.add).then_inc(dist_added, 1)
                    soft = head if kv is not None else head - NA
                    if kv is None:
                        dve.wait_ge(mask_loaded, 16)
                    dve.wait_ge(dist_added, soft)
                    dve.nop(nofuse=True)
                    for m, (lo, hi) in enumerate(((0, P), (P, S384))):
                        last = dve.tensor_tensor_reduce(s_buf[:, b, lo:hi], s_buf[:, b, lo:hi], c["a_mask"][:, lo:hi],
                                                        1.0, -3e38, ALU.add, ALU.max, smax[:, b, m:m + 1])
                    last.then_inc(max_made, 1)
                    dve.wait_ge(max_made, soft)
                    floor = -3e38 if kv is None else sinks[:, slope + h:slope + h + 1]
                    dve.tensor_scalar(nmax[:, b, :], smax[:, b, :], floor, -1.0, ALU.max, ALU.mult).then_inc(s_ready, 1)
                if (what, kind) == ("qk", "stick"):
                    dve.wait_ge(log_ready, head - NA)
                    dve.scalar_tensor_tensor(out=t_buf[:, b, :], in0=work[h % 4][:, 0:S384], scalar=0.0,
                                             in1=s_buf[:, b, :], op0=ALU.max, op1=ALU.add).then_inc(sp_made, 1)
                    dve.wait_ge(sp_made, head - NA)
                    dve.tensor_tensor(t_buf[:, b, :], t_buf[:, b, :], c["b_keep"][:, :],
                                      ALU.mult).then_inc(mid_ready, 1)
                if (what, kind) == ("mid", "stick"):
                    dve.wait_ge(mid_done, head)
                    dve.tensor_tensor(s_buf[:, b, :], work[h % 4][:, 0:S384], c["b_mask"][:, :],
                                      ALU.add).then_inc(s_ready, 1)
                if what == "pv":
                    dve.wait_ge(o_done, head)
                    o = o_nat[:, :, h * HD:(h + 1) * HD]
                    bank = work[2 + b] if kind == "soft" else work[h % 4]
                    src = bank[:, S384:NB].rearrange("p (m d) -> p m d", m=MT)
                if (what, kind) == ("pv", "soft"):
                    if kv is not None:
                        dve.tensor_tensor(den[:, b, :], den[:, b, :], sink_e[:, b, :], ALU.add).then_inc(den_made, 1)
                        dve.wait_ge(den_made, head)
                    dve.reciprocal(rden[:, b, :], den[:, b, :]).then_inc(rden_made, 1)
                    dve.wait_ge(rden_made, head if kv is not None else head - NA)
                    dve.tensor_tensor(o, src, rden[:, b, :].unsqueeze(2).broadcast_to([P, MT, HD]),
                                      ALU.mult).then_inc(o_ready, 1)
                if (what, kind) == ("pv", "stick"):
                    dve.tensor_copy(o, src).then_inc(o_ready, 1)

            def partial(banks, j):
                n = e.n
                dve.wait_ge(half_used, n.half.value())
                dve.wait_ge(sumsq_ready, n.rms.value(unit=JB))
                for m in range(MT):
                    xs = x[:, m, j * NB:(j + 1) * NB]
                    last = dve.tensor_tensor(xs, banks[m][:, :], xs, ALU.add)
                last.then_inc(acc_free[j % 2], 1)

            def residual(banks, halves_behind):
                n = e.n
                j = n.x.c % JB
                dve.wait_ge(half_used, n.half.value(-halves_behind))
                dve.wait_ge(sumsq_ready, n.rms.value(unit=JB))
                for s in range(2):
                    dve.wait_ge(acc_free[s], n.sets[s].value())
                for m in range(MT):
                    xs = x[:, m, j * NB:(j + 1) * NB]
                    last = dve.tensor_tensor(xs, banks[m][:, :], xs, ALU.add)
                last.then_inc(x_ready, 1)

            def up(acc_set):
                n = e.n
                dve.wait_ge(half_used, n.half.value())
                dve.wait_ge(acc_free[0], n.sets[0].value())
                if n.hT.past(1):
                    dve.wait_ge(hT_done, n.hT.value())
                for m in range(MT):
                    last = dve.scalar_tensor_tensor(out=hid[:, m, :], in0=acc[2 * acc_set + m][:, :],
                                                    scalar=rstd[:, m:m + 1], in1=silu_g[:, m, :],
                                                    op0=ALU.mult, op1=ALU.mult)
                last.then_inc(acc_free[acc_set], 1)

            def stage(kt, t):
                dve.wait_ge(shi_ready, e.n.kt.value(1))
                dve.tensor_tensor(stage_lo[:, t, :], hT[:, bass.ds(kt, 1), :].rearrange("p a b -> p (a b)"),
                                  stage_hi[:, t, :].bitcast(F32), ALU.subtract).then_inc(slo_ready, 1)

            e = Steps(first_splits=first_splits, half=lambda **w: split(AHEAD - 1), evacuate_kv=evacuate_kv, xT=xT_low, rms=rms, norm_a=norm_a, norm_b=norm_b,
                      oT=oT, attend=attend, residual=residual, partial=partial, up=up, stage=stage)
            walk(dve, e)

        @block.tensor
        def _(pe):
            def begin():
                pe.wait_ge(gain_loaded, 16 * 3)
                pe.transpose(work[3][:, 0:4 * KT], s_buf[0:4 * KT, 0, 0:P], ident[0:4 * KT, 0:4 * KT]).then_inc(gainT_done, 1)

            def three(out_ps, x_hi, x_lo, wh, wl, start, stop):
                pe.matmul(out_ps, x_hi, wh, start=start, stop=False)
                pe.matmul(out_ps, x_hi, wl, start=False, stop=False)
                return pe.matmul(out_ps, x_lo, wh, start=False, stop=stop)

            def half(src=None, kts=None, acc_set=None, start=False, stop=False, width=NB, needs=None,
                     added=None, down=None, stage=None):
                n = e.n
                s = n.half.slot(SPLIT)
                pe.wait_ge(lo_ready, n.half.value(1))
                if down is None:
                    if start and n.sets[acc_set].past(1):
                        pe.wait_ge(acc_free[acc_set], n.sets[acc_set].value())
                    if start and added is not None:
                        pe.wait_ge(x_ready, added)
                    if needs is not None:
                        pe.wait_ge(*needs)
                    for a, kt in enumerate(kts):
                        wh, wl = (w[:, s, a * width:(a + 1) * width] for w in (w_hi, w_lo))
                        for m in range(MT):
                            rows = slice(m * P, (m + 1) * P)
                            last = three(acc[2 * acc_set + m][:, 0:width], src[0][:, kt, rows], src[1][:, kt, rows],
                                         wh, wl, start and a == 0, stop and a == len(kts) - 1)
                else:
                    if down == 0:
                        pe.wait_ge(slo_ready, n.kt.value())
                    if start:
                        pe.wait_ge(acc_free[down], n.sets[down].value())
                        pe.wait_ge(hT_ready, n.hT.value())
                    for m in range(MT):
                        rows = slice(m * P, (m + 1) * P)
                        for b in range(2):
                            wh, wl = (w[:, s, b * NB:(b + 1) * NB] for w in (w_hi, w_lo))
                            last = three(down_bank[2 * down + b][m][:, :], stage_hi[:, stage, rows],
                                         stage_lo[:, stage, rows], wh, wl, start, stop)
                last.then_inc(half_used, 1)

            def four_by_two(src, banks, tiles=4):
                for t in range(tiles):
                    for m in range(MT):
                        at = (t % 2) * SEQ + m * P
                        last = pe.transpose(banks[t // 2][:, at:at + P], src(m, t), ident[:, :])
                return last

            def xT(gain, j, needs):
                n = e.n
                if needs is None:
                    pe.wait_ge(x_loaded[j], 32)
                else:
                    pe.wait_ge(x_ready, needs)
                if n.xT.c >= 2:
                    pe.wait_ge(xT_ready, n.xT.c - 1)
                if n.xT.c == 1:
                    pe.wait_ge(gains_ready, 1)
                four_by_two(lambda m, t: x[:, m, (4 * j + t) * P:(4 * j + t + 1) * P],
                            work[2 * (j % 2):2 * (j % 2) + 2]).then_inc(xT_done, 1)

            def qkT(src, dst, gain):
                n = e.n
                if gain is None or gain is False:
                    taken_out(pe, n)
                else:
                    pe.wait_ge(normed, n.norm.value())
                if n.head.past(1):
                    pe.wait_ge(o_ready, n.head.value())
                if dst is kT and n.oT.past(1):
                    pe.wait_ge(oT_ready, n.oT.value())
                banks = work[2:4] if dst is kT else work[0:2]
                four_by_two(lambda m, t: src[:, m, t * P:(t + 1) * P], banks,
                            2 if src is k_dup else 4).then_inc(qkT_done, 1)

            def oT(kt0, later):
                n = e.n
                pe.wait_ge(o_ready, n.head.value())
                pe.wait_ge(qkT_ready, n.qkT.value(-later))
                four_by_two(lambda m, t: o_nat[:, m, t * P:(t + 1) * P], work[2:4]).then_inc(oT_done, 1)

            def hidden(j):
                n = e.n
                pe.wait_ge(acc_free[1], n.sets[1].value())
                if n.hT.past(1):
                    pe.wait_ge(hT_ready, n.hT.value())
                four_by_two(lambda m, t: hid[:, m, t * P:(t + 1) * P], work[2:4]).then_inc(hT_done, 1)

            def attend(what, h, kind, slope, kv):
                n, b = e.n, h % 2
                head = n.head.value(h + 1)
                rows = slice(b * HD, (b + 1) * HD)
                bank = work[h % 4]
                if what == "qk" and h == 0:
                    pe.wait_ge(qkT_ready, n.qkT.value())
                    taken_out(pe, n)
                if (what, kind) == ("qk", "soft"):
                    key = h // 2 if kv is None else kv
                    pe.matmul(work[b][:, 0:P], qT[rows, h // 2, 0:P], kT[rows, key, 0:P], start=True, stop=True)
                    pe.matmul(work[b][:, P:S384], qT[rows, h // 2, P:SEQ], kT[rows, key, :],
                              start=True, stop=True).then_inc(s_done, 1)
                if (what, kind) == ("mid", "soft"):
                    pe.wait_ge(mid_ready, head)
                    if h >= 2:
                        pe.wait_ge(o_ready, n.head.value(h - 1))
                    elif n.oT.past(1):
                        pe.wait_ge(oT_ready, n.oT.value())
                    for k in range(3):
                        last = pe.transpose(work[2 + b][:, k * P:(k + 1) * P], p_buf[:, b, k * P:(k + 1) * P],
                                            ident[:, :])
                    last.then_inc(mid_done, 1)
                if (what, kind) == ("qk", "stick"):
                    if h >= 4:
                        pe.wait_ge(o_ready, n.head.value(h - 3))
                    elif h >= 2:
                        pe.wait_ge(oT_ready, n.oT.value())
                    pe.matmul(bank[:, 0:SEQ], kT[rows, h // 2, 0:P], qT[rows, h // 2, :], start=True, stop=False,
                              skip_group_check=True)
                    pe.matmul(bank[:, SEQ:S384], kT[rows, h // 2, P:SEQ], qT[rows, h // 2, P:SEQ], start=False,
                              stop=False, skip_group_check=True).then_inc(s_done, 1)
                if (what, kind) == ("mid", "stick"):
                    pe.wait_ge(mid_ready, head)
                    pe.matmul(bank[:, 0:SEQ], c["tri"][:, :], t_buf[:, b, 0:SEQ], start=False, stop=False,
                              skip_group_check=True)
                    pe.matmul(bank[:, P:SEQ], c["ones"][:, :], t_buf[:, b, SEQ:S384], start=False, stop=False,
                              skip_group_check=True)
                    pe.matmul(bank[:, SEQ:S384], c["tri"][:, :], t_buf[:, b, SEQ:S384], start=False, stop=True,
                              skip_group_check=True).then_inc(mid_done, 1)
                if what == "pv":
                    pe.wait_ge(pt_ready, head)
                    pt, o = (t_buf, work[2 + b]) if kind == "soft" else (p_buf, bank)
                    vs = slice(h * HD, (h + 1) * HD) if kv is None else slice(kv * HD, (kv + 1) * HD)
                    pe.matmul(o[:, S384:S384 + HD], pt[:, b, 0:P], v_nat[:, 0, vs], start=True, stop=True)
                    pe.matmul(o[:, S384 + HD:NB], pt[:, b, P:SEQ], v_nat[:, 0, vs], start=True, stop=False)
                    pe.matmul(o[:, S384 + HD:NB], pt[:, b, SEQ:S384], v_nat[:, 1, vs], start=False,
                              stop=True).then_inc(o_done, 1)

            e = Steps(begin=begin, half=half, xT=xT, qkT=qkT, oT=oT, hidden=hidden, attend=attend)
            walk(pe, e)


_INS = ['x', 'attn_norm', 'ffn_norm', 'even_w_in', 'even_q_norm', 'even_k_norm', 'even_sinks', 'even_w_out',
        'odd_w_in', 'odd_q_norm', 'odd_k_norm', 'odd_w_out', 'ffn_w_gate', 'ffn_w_up', 'ffn_w_down']


def kernel(**inputs):
    import numpy as _np
    import concourse.bacc as _bacc
    from concourse import mybir as _mybir
    from concourse.bass_utils import run_bass_kernel_spmd as _run

    nc = _bacc.Bacc("TRN2", target_bir_lowering=False, num_devices=1)
    consts, widths, c_mask = make_constants(inputs['even_sinks'].shape[1], inputs['x'].shape[2] // HD)
    arrays, args = {}, []
    for name, a in [(name, inputs[name]) for name in _INS] + [('consts', consts), ('c_mask', c_mask)]:
        a = _np.ascontiguousarray(a)
        arrays[f"in_{name}_dram"] = a
        args.append(nc.dram_tensor(f"in_{name}_dram", a.shape, _mybir.dt.from_np(a.dtype), kind="ExternalInput").ap())
    args.append(nc.dram_tensor("out_0_dram", inputs['x'].shape, _mybir.dt.float32, kind="ExternalOutput").ap())
    decoder_kernel(nc, widths, *args)
    r = _run(nc, [arrays], core_ids=[0])
    return r.results[0]["out_0_dram"]
```

```python
from contextlib import ExitStack, contextmanager

import numpy as np

import concourse.bass as bass
from concourse import mybir

F32 = mybir.dt.float32
F32R = mybir.dt.float32r
ALU = mybir.AluOpType
ACT = mybir.ActivationFunctionType
AX_X = mybir.AxisListType.X

P = 128
HD = 64
GROUP = 8
NB = 512
CHUNK = 4 * NB
HALF = CHUNK // 2
RAW = 4
SPLIT = 4
AHEAD = 3
EPS = 1e-6
NEG = -1e30
PLAIN_Q, PLAIN_K = -1, -2
S384 = 3 * P

SLOTS24 = ([1, 3, 5, 7, 10, 12, 15, 17], 2, 4)
SLOTS18 = ([0, 2, 4, 6, 8, 10, 12, 13], 2, 4)
SLOTS16 = ([0, 2, 4, 5, 7, 9, 11, 12], 2, 3)


class Count:

    def __init__(self):
        self.c, self.per, self.i = 0, 0, None

    def past(self, n):
        return self.i is not None or self.c >= n

    def value(self, more=0, unit=1):
        at = (self.c + more) * unit
        return at if self.i is None else self.i * (self.per * unit) + at

    def slot(self, ring, more=0):
        assert self.per % ring == 0
        return (self.c + more) % ring

    def turn(self, ring, more=0, plus=0, unit=1):
        at = ((self.c + more) // ring + plus) * unit
        return at if self.i is None else self.i * (self.per // ring * unit) + at


class Counts:

    def __init__(self):
        self.half = Count()
        self.chunk = Count()
        self.x = Count()
        self.xT = Count()
        self.rms = Count()
        self.norm = Count()
        self.qkT = Count()
        self.head = Count()
        self.oT = Count()
        self.hT = Count()
        self.kt = Count()
        self.sets = [Count(), Count()]

    @contextmanager
    def loop(self, eng, rounds, sets=(0, 0), **per):
        known = {"half": self.half, "chunk": self.chunk, "norm": self.norm, "qkT": self.qkT, "head": self.head,
                 "oT": self.oT, "hT": self.hT, "kt": self.kt}
        every = [(v, per.get(k, 0)) for k, v in known.items()] + list(zip(self.sets, sets))
        start = [v.c for v, _ in every]
        with eng.Fori(0, rounds) as i:
            for v, k in every:
                v.i, v.per = (i, k) if k else (None, 0)
            yield i
            for (v, k), c in zip(every, start):
                assert v.c == c + k, (v.c, c, k)
                v.i, v.c, v.per = None, c + rounds * k, 0


def steps_at(slots, k):
    qk, mid, last = slots
    out = []
    for h in range(GROUP):
        if qk[h] + last == k:
            out.append(("pv", h))
    for h in range(GROUP):
        if qk[h] + mid == k:
            out.append(("mid", h))
    for h in range(GROUP):
        if qk[h] == k:
            out.append(("qk", h))
    return out


def make_constants(n_a, n_c):
    q = np.arange(P)[:, None]
    k = np.arange(P)[None, :]
    dist = np.concatenate([q - k, q + P - k, q - k], 1)
    in_a = (dist >= 0) & (dist < 128)
    count = (((dist >= 0) & (dist <= 128)).astype(int) + ((dist >= 0) & (dist % 4 == 0))
             + ((dist >= 0) & (dist % 16 == 0)))
    c_mask = np.where(count > 0, np.log(np.maximum(count, 1)), NEG)
    keep = np.concatenate([k > q, np.ones((P, P)), k > q], 1)
    parts = {
        "minus_dist": -np.maximum(dist, 0.0),
        "a_mask": np.where(in_a, 0.0, NEG),
        "b_keep": keep,
        "b_mask": np.where(keep > 0, 0.0, NEG),
        "ident": np.eye(P),
        "tri": np.where(q >= k, -1.0, 0.0),
        "ones": np.full((P, P), -1.0),
        "slopes": np.tile(np.concatenate([2.0 ** (-8.0 * np.arange(1, n_a + 1) / n_a),
                                          2.0 ** (-8.0 * np.arange(1, n_c + 1) / n_c)]), (P, 1)),
        "half": np.full((P, 16), -0.5),
    }
    return np.concatenate([v.astype(np.float32) for v in parts.values()], 1), \
        {n: v.shape[1] for n, v in parts.items()}, c_mask.astype(np.float32)


def decoder_kernel(nc, widths, x_in, attn_norm, ffn_norm, even_w_in, even_q_norm, even_k_norm, even_sinks,
                   even_w_out, odd_w_in, odd_q_norm, odd_k_norm, odd_w_out, w_gate, w_up, w_down,
                   consts, c_mask_in, out):
    _, SEQ, D = x_in.shape
    FF = w_gate.shape[2]
    MT = SEQ // P
    KT = D // P
    JB = D // NB
    FB = FF // NB
    FK = FF // P
    NA = even_sinks.shape[1]
    NC = D // HD
    CG = NC // GROUP
    assert MT == 2 and KT == 16 and JB == 4 and NA == 2 * GROUP and FF % NB == 0
    AQ, AK = NA * HD, 2 * HD
    OFF, at = {}, 0
    for name, width in widths.items():
        OFF[name] = at
        at += width
    BIG = ("minus_dist", "a_mask", "b_keep", "b_mask", "tri", "ones")
    CONSTS = len(widths) - 1 - len(BIG) + 8 + 1
    HALVES = 4 + 8 * 8 + 2 * 4 * 8 + 3 * CG * 8 + 2 * (2 * FB * 8 + FK * 2)
    BQ = AQ + 2 * AK

    with ExitStack() as ctx:
        def sb(name, shape, dt, stack=ctx):
            return stack.enter_context(nc.sbuf_tensor(name, shape, dt))

        def sem(name):
            return ctx.enter_context(nc.semaphore(name))

        raw = sb("raw", [P, RAW, CHUNK], F32)
        w_hi = sb("w_hi", [P, SPLIT, HALF], F32R)
        w_lo = sb("w_lo", [P, SPLIT, HALF], F32R)
        x = sb("x", [P, MT, D], F32)
        xT_hi = sb("xT_hi", [P, KT, SEQ], F32R)
        xT_lo = sb("xT_lo", [P, KT, SEQ], F32R)
        s_buf = sb("s_buf", [P, 2, S384], F32)
        p_buf = sb("p_buf", [P, 2, S384], F32)
        t_buf = sb("t_buf", [P, 2, S384], F32)
        c = {n: sb(n, [P, w], F32) for n, w in widths.items()}
        ident = c["ident"]
        gains = sb("gains", [P, 2 * 2 * KT], F32)
        qk_gain = sb("qk_gain", [P, 4], F32)
        sinks = sb("sinks", [P, NA], F32)
        sumsq = sb("sumsq", [P, MT, JB], F32)
        msq = sb("msq", [P, MT], F32)
        rstd = sb("rstd", [P, MT], F32)
        hsum = sb("hsum", [P, MT * GROUP], F32)
        hrstd = sb("hrstd", [P, MT * GROUP], F32)
        smax = sb("smax", [P, 2, 2], F32)
        nmax = sb("nmax", [P, 2, 2], F32)
        den = sb("den", [P, 2, 2], F32)
        sink_e = sb("sink_e", [P, 2, 2], F32)
        rden = sb("rden", [P, 2, 2], F32)
        with ExitStack() as s1:
            hT = sb("hT", [P, FK, SEQ], F32, s1)
            stage_hi = sb("stage_hi", [P, 4, SEQ], F32R, s1)
            stage_lo = sb("stage_lo", [P, 4, SEQ], F32R, s1)
            silu_g = sb("silu_g", [P, MT, NB], F32, s1)
            hid = sb("hid", [P, MT, NB], F32, s1)
        oT_hi = sb("oT_hi", [P, KT, SEQ], F32R)
        oT_lo = sb("oT_lo", [P, KT, SEQ], F32R)
        q_nat = sb("q_nat", [P, MT, NB], F32)
        k_nat = sb("k_nat", [P, MT, NB], F32)
        v_nat = sb("v_nat", [P, MT, NB], F32)
        qT = sb("qT", [P, 4, SEQ], F32)
        kT = sb("kT", [P, 4, SEQ], F32)
        sq = sb("sq", [P, MT, NB], F32)
        o_nat = sb("o_nat", [P, MT, NB], F32)

        acc = [ctx.enter_context(nc.psum_tensor(f"acc{i}", [P, NB], F32)) for i in range(4)]
        work = [ctx.enter_context(nc.psum_tensor(f"work{i}", [P, NB], F32)) for i in range(4)]
        down_bank = [work[0:2], acc[0:2], work[2:4], acc[2:4]]

        raw_loaded = [sem(f"raw_loaded{i}") for i in range(RAW)]
        const_loaded = sem("const_loaded")
        big_loaded = sem("big_loaded")
        x_loaded = [sem(f"x_loaded{j}") for j in range(JB)]
        gain_loaded = sem("gain_loaded")
        mask_loaded = sem("mask_loaded")
        hi_ready = sem("hi_ready")
        lo_ready = sem("lo_ready")
        half_used = sem("half_used")
        acc_free = [sem(f"acc_free{i}") for i in range(2)]
        gainT_done = sem("gainT_done")
        gains_ready = sem("gains_ready")
        x_ready = sem("x_ready")
        xT_done = sem("xT_done")
        xhi_ready = sem("xhi_ready")
        xT_ready = sem("xT_ready")
        sumsq_ready = sem("sumsq_ready")
        msq_ready = sem("msq_ready")
        rstd_ready = sem("rstd_ready")
        hsum_ready = sem("hsum_ready")
        hrstd_ready = sem("hrstd_ready")
        normed = sem("normed")
        qkT_done = sem("qkT_done")
        qkT_ready = sem("qkT_ready")
        s_done = sem("s_done")
        s_ready = sem("s_ready")
        mid_done = sem("mid_done")
        pt_ready = sem("pt_ready")
        log_ready = sem("log_ready")
        mid_ready = sem("mid_ready")
        o_done = sem("o_done")
        o_ready = sem("o_ready")
        oT_done = sem("oT_done")
        ohi_ready = sem("ohi_ready")
        oT_ready = sem("oT_ready")
        hT_done = sem("hT_done")
        hT_ready = sem("hT_ready")
        shi_ready = sem("shi_ready")
        slo_ready = sem("slo_ready")
        abs_ready = sem("abs_ready")
        exp_ready = sem("exp_ready")
        sum_made = sem("sum_made")
        sq_made = sem("sq_made")
        hsum_made = sem("hsum_made")
        dist_added = sem("dist_added")
        max_made = sem("max_made")
        den_made = sem("den_made")
        rden_made = sem("rden_made")
        sp_made = sem("sp_made")
        qgain_made = sem("qgain_made")
        sums_done = sem("sums_done")
        result_ready = sem("result_ready")
        stored = sem("stored")

        def xT_banks(j, pair):
            return (work[0:2], work[2:4], acc[0:2])[j % 2 if pair is None else pair]

        def heads_view(t):
            return t.rearrange("p m (h d) -> p (m h) d", d=HD)

        k_dup = k_nat[:, 0, :].rearrange("p (m n) -> p m n", m=MT)

        def taken_out(eng, n):
            for free, taken in zip(acc_free, n.sets):
                if taken.past(1):
                    eng.wait_ge(free, taken.value())

        def walk(eng, e):
            n = Counts()
            e.n = n
            norm_a = e.norm_a

            def half(**what):
                e.half(**what)
                n.half.c += 1

            def evacuate(dst, acc_set):
                e.evacuate(dst, acc_set)
                n.sets[acc_set].c += 1

            def xT(gain, j, needs=None, pair=None):
                e.xT(gain, j, needs, pair)
                n.xT.c += 1

            def norm_b(t):
                e.norm_b(t)
                n.norm.c += 1

            def qkT(src, dst, gain):
                e.qkT(src, dst, gain)
                n.qkT.c += 1

            def oT(kt0, later=0):
                e.oT(kt0, later)
                n.oT.c += 1

            def attend(slots, k, kind, layer_c=None, kv=None):
                for what, h in steps_at(slots, k):
                    e.attend(what, h, kind, layer_c, kv)
                if k == slots[0][-1] + slots[2]:
                    n.head.c += GROUP

            def block(acc_set, src=(xT_hi, xT_lo), extra=None, first=False, added=None):
                x0 = n.xT.c // JB * JB if n.xT.c % JB else n.xT.c - JB
                for k in range(8):
                    half(src=src, kts=(2 * k, 2 * k + 1), acc_set=acc_set, start=k == 0, stop=k == 7,
                         needs=(xT_ready, x0 + k // 2 + 1) if first else None, added=added)
                    if extra:
                        extra(k)

            def residual(banks):
                e.residual(banks)
                n.x.c += 1

            def down_residual(j, behind=0):
                e.down_residual(j, behind)
                n.x.c += 1

            def rms(step):
                if 0 <= step < JB:
                    e.squares(step)
                if step == JB:
                    e.rms()
                    n.rms.c += 1

            def out_projection(gain, kind, layer_c, first_oT=None):
                src = (oT_hi, oT_lo)
                o0 = n.oT.c // CG * CG
                last = KT // 2 - 2
                k = 0
                for j in range(JB):
                    for cc in range(last):
                        half(src=src, kts=(2 * cc, 2 * cc + 1), acc_set=j % 2, start=cc == 0, stop=cc == last - 1,
                             needs=(oT_ready, o0 + cc // 2 + 1))
                        if k == 0 and first_oT is not None:
                            qkT(q_nat, qT, PLAIN_Q)
                            qkT(k_nat, kT, PLAIN_K)
                        attend(SLOTS24, k, kind, layer_c)
                        if k == 1 and first_oT is not None:
                            oT(first_oT)
                        if k == 22:
                            oT(3 * 4)
                        k += 1
                    e.partial(acc[2 * (j % 2):2 * (j % 2) + 2], j)
                    n.sets[j % 2].c += 1
                x0 = n.x.c
                for j in range(JB):
                    for cc in (last, last + 1):
                        half(src=src, kts=(2 * cc, 2 * cc + 1), acc_set=j % 2, start=cc == last,
                             stop=cc == last + 1, needs=(oT_ready, o0 + 4), added=x0 + j - 1 if j >= 2 else None)
                    residual(acc[2 * (j % 2):2 * (j % 2) + 2])
                    if j >= 1:
                        xT(gain, j - 1, x0 + j)

            def feed_forward(layer):
                x0 = n.x.c

                def with_gate(k):
                    if k == 1:
                        xT(2 + layer, 3, x0)
                    rms(k - 2)
                block(0, extra=with_gate, first=True, added=x0 - 1)
                e.gate(0)
                n.sets[0].c += 1
                block(1, added=x0)
                e.up(1)
                n.sets[1].c += 1

                def hidden(j):
                    e.hidden(j)
                    n.hT.c += 1

                def ff_block(j, extra=None):
                    block(0, extra=lambda k: hidden(j) if k == 2 else None)
                    e.gate(0)
                    n.sets[0].c += 1
                    block(1, extra=extra)
                    e.up(1)
                    n.sets[1].c += 1

                def stage(kt, slot):
                    e.stage(kt, slot)
                    n.kt.c += 1

                with n.loop(eng, FB - 2, half=16, sets=(1, 1), hT=1) as j:
                    ff_block(j)
                ff_block(FB - 2, lambda k: stage(0, 0) if k == 5 else None)

                def rows(at, tiles=4, start=False):
                    for t in range(tiles):
                        half(down=0, stage=t, start=start and t == 0)
                        if start and t == 0:
                            hidden(FB - 1)
                        stage(at + t + 1, (t + 1) % 4)
                        half(down=1, stage=t, start=start and t == 0)

                rows(0, start=True)
                with n.loop(eng, FK // 4 - 2, half=8, kt=4) as j:
                    rows(j * 4 + 4)
                rows(FK - 4, tiles=2)

                x0 = n.x.c
                stage(FK - 1, 3)
                half(down=0, stage=2, staged_since=1)
                half(down=0, stage=3, stop=True)
                down_residual(0)
                down_residual(1)
                half(down=1, stage=2)
                if layer == 0:
                    xT(1, 0, x0 + 2, pair=2)
                half(down=1, stage=3, stop=True)
                down_residual(2)
                if layer == 0:
                    xT(1, 1, x0 + 2, pair=0)
                else:
                    down_residual(3)

            e.begin()
            xT(0, 0)
            e.first_split(0)
            xT(0, 1)
            for k in range(1, AHEAD):
                e.first_split(k)
            for k in range(4):
                if 0 < k < 3:
                    xT(0, k + 1)
                half(src=(xT_hi, xT_lo), kts=range(4 * k, 4 * k + 4), acc_set=1, start=k == 0, stop=k == 3,
                     width=2 * P, needs=(xT_ready, k + 1))
                rms(k - 3)

            def with_a_queries(k):
                rms(k + 1)
                if k == 3:
                    e.evacuate_kv(1)
                    n.sets[1].c += 1
                if k == 4:
                    norm_a(k_dup)
                if k == 6:
                    norm_b(k_dup)
            block(0, extra=with_a_queries)
            evacuate(q_nat, 0)

            def layer0(t):
                if t == 0:
                    norm_a(q_nat)
                if t == 2:
                    norm_b(q_nat)
                if t == 3:
                    qkT(k_dup, kT, 1)
                    qkT(q_nat, qT, 0)
                if 4 <= t < 20:
                    attend(SLOTS16, t - 4, "soft", 0, 0)
                if t == 9:
                    norm_a(q_nat)
                if t == 11:
                    norm_b(q_nat)
                if t == 20:
                    qkT(q_nat, qT, 0)
                    evacuate(q_nat, 0)
                    oT(0, later=2)
                if 21 <= t < 37:
                    attend(SLOTS16, t - 21, "soft", GROUP, 1)
                if t == 36:
                    evacuate(v_nat, 0)
                if t == 37:
                    qkT(q_nat, qT, PLAIN_Q)
                    qkT(k_nat, kT, PLAIN_K)
                if t >= 38:
                    attend(SLOTS18, t - 38, "stick")
                if t == 38:
                    oT(4)

            block(1, extra=layer0)
            evacuate(q_nat, 1)
            block(0, extra=lambda k: layer0(8 + k))
            block(1, extra=lambda k: layer0(16 + k))
            evacuate(k_nat, 1)
            block(0, extra=lambda k: layer0(24 + k))
            block(1, extra=lambda k: layer0(32 + k))
            evacuate(q_nat, 1)
            block(0, extra=lambda k: layer0(40 + k))
            evacuate(k_nat, 0)
            block(1, extra=lambda k: layer0(48 + k))
            evacuate(v_nat, 1)
            out_projection(2, "stick", None, first_oT=8)
            feed_forward(0)

            x0 = n.x.c

            def with_queries(k):
                if k == 0:
                    down_residual(3, 1)
                if k == 1:
                    xT(1, 2, x0, pair=1)
                if k == 3:
                    xT(1, 3, x0 + 1, pair=0)
                rms(k - 2)
            block(0, extra=with_queries, first=True)
            evacuate(q_nat, 0)
            block(1, extra=lambda k: norm_a(q_nat) if k == 1 else norm_b(q_nat) if k == 3 else None)
            evacuate(k_nat, 1)
            block(0, extra=lambda k: norm_a(k_nat) if k == 1 else norm_b(k_nat) if k == 3 else None)
            evacuate(v_nat, 0)
            qkT(q_nat, qT, 2)
            qkT(k_nat, kT, 3)
            with n.loop(eng, CG - 1, half=24, norm=2, qkT=2, head=GROUP, oT=1, sets=(2, 1)) as g:
                slope0 = g * GROUP + NA
                block(0, extra=lambda k: attend(SLOTS24, k, "soft", slope0))
                evacuate(q_nat, 0)

                def c2(k):
                    attend(SLOTS24, k + 8, "soft", slope0)
                    if k == 1:
                        norm_a(q_nat)
                    if k == 3:
                        norm_b(q_nat)
                block(1, extra=c2)
                evacuate(k_nat, 1)

                def c3(k):
                    attend(SLOTS24, k + 16, "soft", slope0)
                    if k == 1:
                        norm_a(k_nat)
                    if k == 3:
                        norm_b(k_nat)
                    if k == 6:
                        qkT(q_nat, qT, 2)
                        oT(g * 4, later=1)
                block(0, extra=c3)
                evacuate(v_nat, 0)
                qkT(k_nat, kT, 3)
            out_projection(3, "soft", NA + (CG - 1) * GROUP)
            feed_forward(1)

        def nothing(*args, **named):
            return None

        class Steps:

            def __init__(self, begin=nothing, first_split=nothing, half=nothing, evacuate=nothing,
                         evacuate_kv=nothing, xT=nothing, norm_a=nothing, norm_b=nothing, qkT=nothing, oT=nothing,
                         attend=nothing, partial=nothing, residual=nothing, down_residual=nothing,
                         squares=nothing, rms=nothing, gate=nothing, up=nothing, hidden=nothing, stage=nothing):
                self.n, self.begin, self.first_split = None, begin, first_split
                self.half, self.evacuate, self.evacuate_kv, self.xT = half, evacuate, evacuate_kv, xT
                self.norm_a, self.norm_b, self.qkT, self.oT, self.attend = norm_a, norm_b, qkT, oT, attend
                self.partial, self.residual, self.down_residual = partial, residual, down_residual
                self.squares, self.rms = squares, rms
                self.gate, self.up, self.hidden, self.stage = gate, up, hidden, stage

        block = ctx.enter_context(nc.Block())

        @block.sync
        def _(sp):
            n = Counts()

            def chunk(src, tiles=None):
                if n.chunk.past(RAW):
                    sp.wait_ge(lo_ready, n.chunk.value(1 - RAW, unit=2))
                s = n.chunk.slot(RAW)
                dst = raw[:, s, :]
                if tiles:
                    dst = dst.rearrange("p (t n) -> p t n", t=tiles)
                sp.dma_start(dst, src).then_inc(raw_loaded[s], 16)
                n.chunk.c += 1

            def columns(w, cols, which=range(KT // 4)):
                wv = w.rearrange("(c t p) n -> c p t n", t=4, p=P)
                for k in which:
                    chunk(wv[k][:, :, cols], 4)

            def out_projection(w):
                for which in (range(3), [3]):
                    for j in range(JB):
                        columns(w, slice(j * NB, (j + 1) * NB), which)

            def feed_forward(layer):
                with n.loop(sp, FB, chunk=8) as j:
                    columns(w_gate[layer], bass.ds(j * NB, NB))
                    columns(w_up[layer], bass.ds(j * NB, NB))
                with n.loop(sp, FK // 4 - 1, chunk=4) as j:
                    for t in range(4):
                        chunk(w_down[layer][bass.ds(j * (4 * P) + t * P, P), :])
                for t in (FK - 4, FK - 3):
                    chunk(w_down[layer][t * P:(t + 1) * P, :])
                rest = w_down[layer][(FK - 2) * P:, :].rearrange("(t p) n -> p t n", p=P)
                for b in range(2):
                    chunk(rest[:, :, b * HALF:(b + 1) * HALF], 2)

            kv = even_w_in[0].rearrange("(c t p) n -> c p t n", t=8, p=P)
            for j in range(JB):
                for m in range(MT):
                    sp.dma_start(x[:, m, j * NB:(j + 1) * NB],
                                 x_in[0, m * P:(m + 1) * P, j * NB:(j + 1) * NB]).then_inc(x_loaded[j], 16)
                if j == 0:
                    sp.dma_start(ident[:, :], consts[:, OFF["ident"]:OFF["ident"] + P]).then_inc(gain_loaded, 16)
                if j in (0, JB - 1):
                    chunk(kv[j // 2][:, :, AQ:AQ + 2 * AK], 8)
            columns(even_w_in[0], slice(0, NB), range(2))
            for name in BIG:
                sp.dma_start(c[name][:, :], consts[:, OFF[name]:OFF[name] + widths[name]]).then_inc(big_loaded, 16)
            columns(even_w_in[0], slice(0, NB), range(2, KT // 4))
            for first in [NB] + [BQ + t * AQ + g * NB for g in range(2) for t in range(3)]:
                columns(even_w_in[0], slice(first, first + NB))
            out_projection(even_w_out[0])
            feed_forward(0)
            sp.wait_ge(s_ready, 2 * GROUP)
            sp.dma_start(c["a_mask"][:, :], c_mask_in).then_inc(mask_loaded, 16)
            with n.loop(sp, CG, chunk=12) as g:
                for t in range(3):
                    columns(odd_w_in[0], bass.ds(g * NB + t * D, NB))
            out_projection(odd_w_out[0])
            feed_forward(1)
            for j in range(JB):
                for m in range(MT):
                    sp.wait_ge(result_ready, j * MT + m + 1)
                    sp.dma_start(out[0, m * P:(m + 1) * P, j * NB:(j + 1) * NB],
                                 x[:, m, j * NB:(j + 1) * NB]).then_inc(stored, 16)
            sp.wait_ge(stored, 16 * JB * MT)

        @block.gpsimd
        def _(pool):
            def begin():
                for name in widths:
                    if name not in BIG and name != "ident":
                        pool.dma_start(c[name][:, :],
                                       consts[:, OFF[name]:OFF[name] + widths[name]]).then_inc(const_loaded, 16)
                for col, g in enumerate((even_q_norm, even_k_norm, odd_q_norm, odd_k_norm)):
                    for r in range(2):
                        pool.dma_start(qk_gain[r * HD:(r + 1) * HD, col:col + 1],
                                       g.rearrange("a d -> d a")).then_inc(const_loaded, 16)
                pool.dma_start(sinks[:, :], even_sinks[0:1, :].broadcast_to([P, NA])).then_inc(const_loaded, 16)
                pool.wait_ge(const_loaded, 16 * CONSTS)

            def rms():
                pool.wait_ge(msq_ready, e.n.rms.value(1))
                pool.tensor_tensor(rstd[:, :], msq[:, :], c["half"][:, 0:MT], ALU.pow).then_inc(rstd_ready, 1)

            def norm_b(t):
                pool.wait_ge(hsum_ready, e.n.norm.value(1))
                w = GROUP if t is k_dup else MT * GROUP
                pool.tensor_tensor(hrstd[:, 0:w], hsum[:, 0:w], c["half"][:, 0:w], ALU.pow).then_inc(hrstd_ready, 1)

            e = Steps(begin=begin, rms=rms, norm_b=norm_b)
            walk(pool, e)

        @block.scalar
        def _(act):
            def split(more):
                n = e.n
                if n.half.i is None and n.half.c + more >= HALVES:
                    return
                s, r = n.half.slot(SPLIT, more), n.half.slot(2 * RAW, more)
                act.wait_ge(raw_loaded[r // 2], n.half.turn(2 * RAW, more, plus=1, unit=16))
                if n.half.i is not None or n.half.c + more >= SPLIT:
                    act.wait_ge(half_used, n.half.value(more + 1 - SPLIT))
                act.activation(w_hi[:, s, :], raw[:, r // 2, (r % 2) * HALF:(r % 2 + 1) * HALF],
                               ACT.Copy).then_inc(hi_ready, 1)

            def begin():
                for r, g in ((0, attn_norm), (2 * KT, ffn_norm)):
                    act.dma_start(s_buf[r:r + 2 * KT, 0, 0:P],
                                  g.rearrange("l (t p) -> (l t) p", p=P)).then_inc(gain_loaded, 16)
                act.wait_ge(gainT_done, 1)
                act.activation(gains[:, :], work[3][:, 0:4 * KT], ACT.Copy).then_inc(gains_ready, 1)
                act.wait_ge(gains_ready, 1)


            def evacuate(dst, acc_set):
                n = e.n
                act.wait_ge(half_used, n.half.value())
                act.wait_ge(rstd_ready, n.rms.value())
                if dst is v_nat:
                    act.wait_ge(o_done, n.head.value())
                elif n.qkT.past(1):
                    act.wait_ge(qkT_done, n.qkT.value())
                for m in range(MT):
                    last = act.activation(dst[:, m, :], acc[2 * acc_set + m][:, :], ACT.Copy, scale=rstd[:, m:m + 1])
                last.then_inc(acc_free[acc_set], 1)

            def evacuate_kv(acc_set):
                act.wait_ge(half_used, e.n.half.value())
                act.wait_ge(rstd_ready, 1)
                for m in range(MT):
                    for g in range(2):
                        for r in range(2):
                            act.activation(k_dup[:, m, (2 * g + r) * HD:(2 * g + r + 1) * HD],
                                           acc[2 * acc_set + m][:, g * HD:(g + 1) * HD], ACT.Copy,
                                           scale=rstd[:, m:m + 1])
                    last = act.activation(v_nat[:, m, 0:AK], acc[2 * acc_set + m][:, AK:2 * AK], ACT.Copy,
                                          scale=rstd[:, m:m + 1])
                last.then_inc(acc_free[acc_set], 1)

            def xT_high(gain, j, needs, pair):
                act.wait_ge(xT_done, e.n.xT.value(1))
                for t in range(4):
                    kt = 4 * j + t
                    last = act.activation(xT_hi[:, kt, :],
                                          xT_banks(j, pair)[t // 2][:, (t % 2) * SEQ:(t % 2 + 1) * SEQ],
                                          ACT.Copy, scale=gains[:, gain * KT + kt:gain * KT + kt + 1])
                last.then_inc(xhi_ready, 1)

            def squares(j):
                n = e.n
                if n.rms.c == 0:
                    act.wait_ge(x_loaded[j], 32)
                else:
                    act.wait_ge(x_ready, n.x.c - JB + j + 1)
                if n.rms.c or j:
                    act.wait_ge(sumsq_ready, n.rms.c * JB + j)
                for m in range(MT):
                    waste = (t_buf, p_buf)[m][:, :, :].rearrange("p a b -> p (a b)")[:, 0:NB]
                    last = act.activation(waste, x[:, m, j * NB:(j + 1) * NB], ACT.Square,
                                          accum_out=sumsq[:, m, j:j + 1])
                last.then_inc(sumsq_ready, 1)

            def qkT(src, dst, gain):
                act.wait_ge(qkT_done, e.n.qkT.value(1))
                if e.n.qkT.c == 0 and e.n.qkT.i is None:
                    act.wait_ge(qgain_made, 1)
                banks = work[2:4] if dst is kT else work[0:2]
                if src is k_dup:
                    banks = banks[0:1]
                scale = {PLAIN_Q: HD ** -0.5, PLAIN_K: 1.0}[gain] if gain < 0 else qk_gain[:, gain:gain + 1]
                for b, bank in enumerate(banks):
                    last = act.activation(dst[:, 2 * b:2 * b + 2, :].rearrange("p a b -> p (a b)"), bank[:, :],
                                          ACT.Copy, scale=scale)
                last.then_inc(qkT_ready, 1)

            def oT(kt0, later):
                act.wait_ge(oT_done, e.n.oT.value(1))
                for b in range(2):
                    last = act.activation(oT_hi[:, bass.ds(kt0 + 2 * b, 2), :].rearrange("p a b -> p (a b)"),
                                          work[2 + b][:, :], ACT.Copy)
                last.then_inc(ohi_ready, 1)

            def attend(what, h, kind, slope, kv):
                n, b = e.n, h % 2
                head = n.head.value(h + 1)
                if (what, kind) == ("qk", "soft"):
                    act.wait_ge(s_ready, head)
                    for m, (lo, hi) in enumerate(((0, P), (P, S384))):
                        last = act.activation(p_buf[:, b, lo:hi], s_buf[:, b, lo:hi], ACT.Exp,
                                              bias=nmax[:, b, m:m + 1], accum_out=den[:, b, m:m + 1])
                    if kv is not None:
                        last = act.activation(sink_e[:, b, :], nmax[:, b, :], ACT.Exp,
                                              bias=sinks[:, slope + h:slope + h + 1])
                    last.then_inc(mid_ready, 1)
                if (what, kind) == ("mid", "soft"):
                    act.wait_ge(mid_done, head)
                    if n.head.past(2) or h >= 2:
                        act.wait_ge(o_done, n.head.value(h - 1))
                    act.activation(t_buf[:, b, :], work[2 + b][:, 0:S384], ACT.Copy).then_inc(pt_ready, 1)
                if (what, kind) == ("qk", "stick"):
                    act.wait_ge(s_done, head)
                    k = head - NA
                    act.activation(s_buf[:, b, :], work[h % 4][:, 0:S384], ACT.Abs).then_inc(abs_ready, 1)
                    act.wait_ge(abs_ready, k)
                    act.activation(s_buf[:, b, :], s_buf[:, b, :], ACT.Exp, scale=-1.0).then_inc(exp_ready, 1)
                    act.wait_ge(exp_ready, k)
                    act.activation(s_buf[:, b, :], s_buf[:, b, :], ACT.Ln, bias=1.0).then_inc(log_ready, 1)
                if (what, kind) == ("mid", "stick"):
                    act.wait_ge(s_ready, head)
                    act.wait_ge(o_done, n.head.value(h - 1))
                    act.activation(p_buf[:, b, :], s_buf[:, b, :], ACT.Exp).then_inc(pt_ready, 1)

            def gate(acc_set):
                n = e.n
                act.wait_ge(half_used, n.half.value())
                act.wait_ge(rstd_ready, n.rms.value())
                if n.sets[1].past(1):
                    act.wait_ge(acc_free[1], n.sets[1].value())
                for m in range(MT):
                    last = act.activation(silu_g[:, m, :], acc[2 * acc_set + m][:, :], ACT.Silu,
                                          scale=rstd[:, m:m + 1])
                last.then_inc(acc_free[acc_set], 1)

            def hidden(j):
                act.wait_ge(hT_done, e.n.hT.value(1))
                for b in range(2):
                    last = act.activation(hT[:, bass.ds(j * 4 + 2 * b, 2), :].rearrange("p a b -> p (a b)"),
                                          work[2 + b][:, :], ACT.Copy)
                last.then_inc(hT_ready, 1)

            def stage(kt, t):
                n = e.n
                act.wait_ge(hT_ready, n.hT.value())
                if n.kt.past(4):
                    act.wait_ge(half_used, n.half.value(-4))
                act.activation(stage_hi[:, t, :], hT[:, bass.ds(kt, 1), :].rearrange("p a b -> p (a b)"),
                               ACT.Copy).then_inc(shi_ready, 1)

            e = Steps(begin=begin, first_split=split, half=lambda **w: split(AHEAD), evacuate=evacuate,
                      evacuate_kv=evacuate_kv, xT=xT_high, squares=squares, qkT=qkT, oT=oT, attend=attend,
                      gate=gate, hidden=hidden, stage=stage)
            walk(act, e)

        @block.vector
        def _(dve):
            def split(more):
                n = e.n
                if n.half.i is None and n.half.c + more >= HALVES:
                    return
                s, r = n.half.slot(SPLIT, more), n.half.slot(2 * RAW, more)
                dve.wait_ge(hi_ready, n.half.value(more + 1))
                dve.tensor_tensor(w_lo[:, s, :], raw[:, r // 2, (r % 2) * HALF:(r % 2 + 1) * HALF],
                                  w_hi[:, s, :].bitcast(F32), ALU.subtract).then_inc(lo_ready, 1)

            def first_split(k):
                if k < AHEAD - 1:
                    split(k)

            def evacuate_kv(acc_set):
                dve.wait_ge(const_loaded, 16 * CONSTS)
                for col in (0, 2):
                    last = dve.tensor_scalar(qk_gain[:, col:col + 1], qk_gain[:, col:col + 1], HD ** -0.5, None,
                                             ALU.mult)
                last.then_inc(qgain_made, 1)

            def xT_low(gain, j, needs, pair):
                dve.wait_ge(xhi_ready, e.n.xT.value(1))
                for t in range(4):
                    kt = 4 * j + t
                    last = dve.scalar_tensor_tensor(
                        out=xT_lo[:, kt, :], in0=xT_banks(j, pair)[t // 2][:, (t % 2) * SEQ:(t % 2 + 1) * SEQ],
                        scalar=gains[:, gain * KT + kt:gain * KT + kt + 1], in1=xT_hi[:, kt, :].bitcast(F32),
                        op0=ALU.mult, op1=ALU.subtract)
                last.then_inc(xT_ready, 1)

            def rms():
                k = e.n.rms.value(1)
                dve.wait_ge(sumsq_ready, k * JB)
                dve.tensor_reduce(msq[:, :], sumsq[:, :, :], AX_X, ALU.add).then_inc(sum_made, 1)
                dve.wait_ge(sum_made, k)
                dve.tensor_scalar(msq[:, :], msq[:, :], 1.0 / D, EPS, ALU.mult, ALU.add).then_inc(msq_ready, 1)

            def norm_a(t):
                k = e.n.norm.value(1)
                v = heads_view(t)
                w = v.shape[1]
                sqv = sq[:, :, :].rearrange("p m n -> p (m n)")[:, 0:w * HD].rearrange("p (h d) -> p h d", d=HD)
                taken_out(dve, e.n)
                dve.tensor_tensor(sqv, v, v, ALU.mult).then_inc(sq_made, 1)
                dve.wait_ge(sq_made, k)
                dve.tensor_reduce(hsum[:, 0:w], sqv, AX_X, ALU.add).then_inc(hsum_made, 1)
                dve.wait_ge(hsum_made, k)
                dve.tensor_scalar(hsum[:, 0:w], hsum[:, 0:w], 1.0 / HD, EPS, ALU.mult, ALU.add).then_inc(hsum_ready, 1)

            def norm_b(t):
                v = heads_view(t)
                w = v.shape[1]
                dve.wait_ge(hrstd_ready, e.n.norm.value(1))
                dve.tensor_tensor(v, v, hrstd[:, 0:w].unsqueeze(2).broadcast_to([P, w, HD]),
                                  ALU.mult).then_inc(normed, 1)

            def oT(kt0, later):
                dve.wait_ge(ohi_ready, e.n.oT.value(1))
                for b in range(2):
                    at = bass.ds(kt0 + 2 * b, 2)
                    last = dve.tensor_tensor(oT_lo[:, at, :].rearrange("p a b -> p (a b)"), work[2 + b][:, :],
                                             oT_hi[:, at, :].rearrange("p a b -> p (a b)").bitcast(F32), ALU.subtract)
                last.then_inc(oT_ready, 1)

            def attend(what, h, kind, slope, kv):
                n, b = e.n, h % 2
                head = n.head.value(h + 1)
                if (what, kind) == ("qk", "soft"):
                    at = bass.ds(slope + h, 1)
                    if kv == 0 and h == 0:
                        dve.wait_ge(big_loaded, 16 * len(BIG))
                    dve.wait_ge(s_done, head)
                    dve.scalar_tensor_tensor(out=s_buf[:, b, :], in0=c["minus_dist"][:, :], scalar=c["slopes"][:, at],
                                             in1=work[b][:, 0:S384], op0=ALU.mult, op1=ALU.add).then_inc(dist_added, 1)
                    soft = head if kv is not None else head - NA
                    if kv is None:
                        dve.wait_ge(mask_loaded, 16)
                    dve.wait_ge(dist_added, soft)
                    dve.nop(nofuse=True)
                    for m, (lo, hi) in enumerate(((0, P), (P, S384))):
                        last = dve.tensor_tensor_reduce(s_buf[:, b, lo:hi], s_buf[:, b, lo:hi], c["a_mask"][:, lo:hi],
                                                        1.0, -3e38, ALU.add, ALU.max, smax[:, b, m:m + 1])
                    last.then_inc(max_made, 1)
                    dve.wait_ge(max_made, soft)
                    floor = -3e38 if kv is None else sinks[:, slope + h:slope + h + 1]
                    dve.tensor_scalar(nmax[:, b, :], smax[:, b, :], floor, -1.0, ALU.max, ALU.mult).then_inc(s_ready, 1)
                if (what, kind) == ("qk", "stick"):
                    dve.wait_ge(log_ready, head - NA)
                    dve.scalar_tensor_tensor(out=t_buf[:, b, :], in0=work[h % 4][:, 0:S384], scalar=0.0,
                                             in1=s_buf[:, b, :], op0=ALU.max, op1=ALU.add).then_inc(sp_made, 1)
                    dve.wait_ge(sp_made, head - NA)
                    dve.tensor_tensor(t_buf[:, b, :], t_buf[:, b, :], c["b_keep"][:, :],
                                      ALU.mult).then_inc(mid_ready, 1)
                if (what, kind) == ("mid", "stick"):
                    dve.wait_ge(mid_done, head)
                    dve.tensor_tensor(s_buf[:, b, :], work[h % 4][:, 0:S384], c["b_mask"][:, :],
                                      ALU.add).then_inc(s_ready, 1)
                if what == "pv":
                    dve.wait_ge(o_done, head)
                    o = o_nat[:, :, h * HD:(h + 1) * HD]
                    bank = work[2 + b] if kind == "soft" else work[h % 4]
                    src = bank[:, S384:NB].rearrange("p (m d) -> p m d", m=MT)
                if (what, kind) == ("pv", "soft"):
                    if kv is not None:
                        dve.tensor_tensor(den[:, b, :], den[:, b, :], sink_e[:, b, :], ALU.add).then_inc(den_made, 1)
                        dve.wait_ge(den_made, head)
                    dve.reciprocal(rden[:, b, :], den[:, b, :]).then_inc(rden_made, 1)
                    dve.wait_ge(rden_made, head if kv is not None else head - NA)
                    dve.tensor_tensor(o, src, rden[:, b, :].unsqueeze(2).broadcast_to([P, MT, HD]),
                                      ALU.mult).then_inc(o_ready, 1)
                if (what, kind) == ("pv", "stick"):
                    dve.tensor_copy(o, src).then_inc(o_ready, 1)

            def partial(banks, j):
                n = e.n
                dve.wait_ge(half_used, n.half.value())
                dve.wait_ge(sumsq_ready, n.rms.value(unit=JB))
                for m in range(MT):
                    xs = x[:, m, j * NB:(j + 1) * NB]
                    last = dve.tensor_tensor(xs, banks[m][:, :], xs, ALU.add)
                last.then_inc(acc_free[j % 2], 1)

            def residual(banks):
                n = e.n
                j = n.x.c % JB
                dve.wait_ge(half_used, n.half.value())
                for s in range(2):
                    dve.wait_ge(acc_free[s], n.sets[s].value())
                for m in range(MT):
                    xs = x[:, m, j * NB:(j + 1) * NB]
                    last = dve.tensor_tensor(xs, banks[m][:, :], xs, ALU.add)
                last.then_inc(x_ready, 1)

            def down_residual(j, behind):
                n = e.n
                final = n.x.c >= 3 * JB
                halves = n.x.c // (2 * JB) * 2 + j // 2
                dve.wait_ge(sumsq_ready, n.rms.value(unit=JB))
                for m in range(MT):
                    at = MT * (j % 2) + m
                    if at < 2 * MT - 1:
                        dve.wait_ge(sums_done, halves * (2 * MT - 1) + at + 1)
                    else:
                        dve.wait_ge(half_used, n.half.value(-behind))
                    xs = x[:, m, j * NB:(j + 1) * NB]
                    last = dve.tensor_tensor(xs, down_bank[j][m][:, :], xs, ALU.add)
                    if final:
                        last.then_inc(result_ready, 1)
                if not final:
                    last.then_inc(x_ready, 1)

            def up(acc_set):
                n = e.n
                dve.wait_ge(half_used, n.half.value())
                dve.wait_ge(acc_free[0], n.sets[0].value())
                if n.hT.past(1):
                    dve.wait_ge(hT_done, n.hT.value())
                for m in range(MT):
                    last = dve.scalar_tensor_tensor(out=hid[:, m, :], in0=acc[2 * acc_set + m][:, :],
                                                    scalar=rstd[:, m:m + 1], in1=silu_g[:, m, :],
                                                    op0=ALU.mult, op1=ALU.mult)
                last.then_inc(acc_free[acc_set], 1)

            def stage(kt, t):
                dve.wait_ge(shi_ready, e.n.kt.value(1))
                dve.tensor_tensor(stage_lo[:, t, :], hT[:, bass.ds(kt, 1), :].rearrange("p a b -> p (a b)"),
                                  stage_hi[:, t, :].bitcast(F32), ALU.subtract).then_inc(slo_ready, 1)

            e = Steps(first_split=first_split, half=lambda **w: split(AHEAD - 1), evacuate_kv=evacuate_kv, xT=xT_low,
                      rms=rms, norm_a=norm_a, norm_b=norm_b, oT=oT, attend=attend, partial=partial,
                      residual=residual, down_residual=down_residual, up=up, stage=stage)
            walk(dve, e)

        @block.tensor
        def _(pe):
            def begin():
                pe.wait_ge(gain_loaded, 16 * 3)
                pe.transpose(work[3][:, 0:4 * KT], s_buf[0:4 * KT, 0, 0:P],
                             ident[0:4 * KT, 0:4 * KT]).then_inc(gainT_done, 1)

            def three(out_ps, x_hi, x_lo, wh, wl, start, stop):
                pe.matmul(out_ps, x_hi, wh, start=start, stop=False)
                pe.matmul(out_ps, x_hi, wl, start=False, stop=False)
                return pe.matmul(out_ps, x_lo, wh, start=False, stop=stop)

            def half(src=None, kts=None, acc_set=None, start=False, stop=False, width=NB, needs=None,
                     added=None, down=None, stage=None, staged_since=0):
                n = e.n
                s = n.half.slot(SPLIT)
                pe.wait_ge(lo_ready, n.half.value(1))
                if down is None:
                    if start and n.sets[acc_set].past(1):
                        pe.wait_ge(acc_free[acc_set], n.sets[acc_set].value())
                    if start and added is not None:
                        pe.wait_ge(x_ready, added)
                    if needs is not None:
                        pe.wait_ge(*needs)
                    for a, kt in enumerate(kts):
                        wh, wl = (w[:, s, a * width:(a + 1) * width] for w in (w_hi, w_lo))
                        for m in range(MT):
                            rows = slice(m * P, (m + 1) * P)
                            last = three(acc[2 * acc_set + m][:, 0:width], src[0][:, kt, rows], src[1][:, kt, rows],
                                         wh, wl, start and a == 0, stop and a == len(kts) - 1)
                else:
                    if down == 0:
                        pe.wait_ge(slo_ready, n.kt.value(-staged_since))
                    if start:
                        pe.wait_ge(acc_free[down], n.sets[down].value())
                    for b in (1, 0) if start else (0, 1):
                        if start and (down, b) == (1, 0):
                            pe.wait_ge(hT_ready, n.hT.value())
                        wh, wl = (w[:, s, b * NB:(b + 1) * NB] for w in (w_hi, w_lo))
                        for m in range(MT):
                            rows = slice(m * P, (m + 1) * P)
                            last = three(down_bank[2 * down + b][m][:, :], stage_hi[:, stage, rows],
                                         stage_lo[:, stage, rows], wh, wl, start, stop)
                            if stop and (b, m) != (1, MT - 1):
                                last.then_inc(sums_done, 1)
                last.then_inc(half_used, 1)

            def four_by_two(src, banks, tiles=4):
                for t in range(tiles):
                    for m in range(MT):
                        at = (t % 2) * SEQ + m * P
                        last = pe.transpose(banks[t // 2][:, at:at + P], src(m, t), ident[:, :])
                return last

            def xT(gain, j, needs, pair):
                n = e.n
                if needs is None:
                    pe.wait_ge(x_loaded[j], 32)
                else:
                    pe.wait_ge(x_ready, needs)
                if n.xT.c >= 2:
                    pe.wait_ge(xT_ready, n.xT.c - 1)
                if n.xT.c == 1:
                    pe.wait_ge(gains_ready, 1)
                four_by_two(lambda m, t: x[:, m, (4 * j + t) * P:(4 * j + t + 1) * P],
                            xT_banks(j, pair)).then_inc(xT_done, 1)

            def qkT(src, dst, gain):
                n = e.n
                if gain < 0:
                    taken_out(pe, n)
                else:
                    pe.wait_ge(normed, n.norm.value())
                if n.head.past(1):
                    pe.wait_ge(o_ready, n.head.value())
                if dst is kT and n.oT.past(1):
                    pe.wait_ge(oT_ready, n.oT.value())
                banks = work[2:4] if dst is kT else work[0:2]
                four_by_two(lambda m, t: src[:, m, t * P:(t + 1) * P], banks,
                            2 if src is k_dup else 4).then_inc(qkT_done, 1)

            def oT(kt0, later):
                n = e.n
                pe.wait_ge(o_ready, n.head.value())
                pe.wait_ge(qkT_ready, n.qkT.value(-later))
                four_by_two(lambda m, t: o_nat[:, m, t * P:(t + 1) * P], work[2:4]).then_inc(oT_done, 1)

            def hidden(j):
                n = e.n
                pe.wait_ge(acc_free[1], n.sets[1].value())
                if n.hT.past(1):
                    pe.wait_ge(hT_ready, n.hT.value())
                four_by_two(lambda m, t: hid[:, m, t * P:(t + 1) * P], work[2:4]).then_inc(hT_done, 1)

            def attend(what, h, kind, slope, kv):
                n, b = e.n, h % 2
                head = n.head.value(h + 1)
                rows = slice(b * HD, (b + 1) * HD)
                bank = work[h % 4]
                if what == "qk" and h == 0:
                    pe.wait_ge(qkT_ready, n.qkT.value())
                    taken_out(pe, n)
                if (what, kind) == ("qk", "soft"):
                    key = h // 2 if kv is None else kv
                    pe.matmul(work[b][:, 0:P], qT[rows, h // 2, 0:P], kT[rows, key, 0:P], start=True, stop=True)
                    pe.matmul(work[b][:, P:S384], qT[rows, h // 2, P:SEQ], kT[rows, key, :],
                              start=True, stop=True).then_inc(s_done, 1)
                if (what, kind) == ("mid", "soft"):
                    pe.wait_ge(mid_ready, head)
                    if h >= 2:
                        pe.wait_ge(o_ready, n.head.value(h - 1))
                    elif n.oT.past(1):
                        pe.wait_ge(oT_ready, n.oT.value())
                    for k in range(3):
                        last = pe.transpose(work[2 + b][:, k * P:(k + 1) * P], p_buf[:, b, k * P:(k + 1) * P],
                                            ident[:, :])
                    last.then_inc(mid_done, 1)
                if (what, kind) == ("qk", "stick"):
                    if h >= 4:
                        pe.wait_ge(o_ready, n.head.value(h - 3))
                    elif h >= 2:
                        pe.wait_ge(oT_ready, n.oT.value())
                    pe.matmul(bank[:, 0:SEQ], kT[rows, h // 2, 0:P], qT[rows, h // 2, :], start=True, stop=False,
                              skip_group_check=True)
                    pe.matmul(bank[:, SEQ:S384], kT[rows, h // 2, P:SEQ], qT[rows, h // 2, P:SEQ], start=False,
                              stop=False, skip_group_check=True).then_inc(s_done, 1)
                if (what, kind) == ("mid", "stick"):
                    pe.wait_ge(mid_ready, head)
                    pe.matmul(bank[:, 0:SEQ], c["tri"][:, :], t_buf[:, b, 0:SEQ], start=False, stop=False,
                              skip_group_check=True)
                    pe.matmul(bank[:, P:SEQ], c["ones"][:, :], t_buf[:, b, SEQ:S384], start=False, stop=False,
                              skip_group_check=True)
                    pe.matmul(bank[:, SEQ:S384], c["tri"][:, :], t_buf[:, b, SEQ:S384], start=False, stop=True,
                              skip_group_check=True).then_inc(mid_done, 1)
                if what == "pv":
                    pe.wait_ge(pt_ready, head)
                    pt, o = (t_buf, work[2 + b]) if kind == "soft" else (p_buf, bank)
                    vs = slice(h * HD, (h + 1) * HD) if kv is None else slice(kv * HD, (kv + 1) * HD)
                    pe.matmul(o[:, S384:S384 + HD], pt[:, b, 0:P], v_nat[:, 0, vs], start=True, stop=True)
                    pe.matmul(o[:, S384 + HD:NB], pt[:, b, P:SEQ], v_nat[:, 0, vs], start=True, stop=False)
                    pe.matmul(o[:, S384 + HD:NB], pt[:, b, SEQ:S384], v_nat[:, 1, vs], start=False,
                              stop=True).then_inc(o_done, 1)

            e = Steps(begin=begin, half=half, xT=xT, qkT=qkT, oT=oT, hidden=hidden, attend=attend)
            walk(pe, e)


_INS = ['x', 'attn_norm', 'ffn_norm', 'even_w_in', 'even_q_norm', 'even_k_norm', 'even_sinks', 'even_w_out',
        'odd_w_in', 'odd_q_norm', 'odd_k_norm', 'odd_w_out', 'ffn_w_gate', 'ffn_w_up', 'ffn_w_down']


def kernel(**inputs):
    import numpy as _np
    import concourse.bacc as _bacc
    from concourse import mybir as _mybir
    from concourse.bass_utils import run_bass_kernel_spmd as _run

    nc = _bacc.Bacc("TRN2", target_bir_lowering=False, num_devices=1)
    consts, widths, c_mask = make_constants(inputs['even_sinks'].shape[1], inputs['x'].shape[2] // HD)
    arrays, args = {}, []
    for name, a in [(name, inputs[name]) for name in _INS] + [('consts', consts), ('c_mask', c_mask)]:
        a = _np.ascontiguousarray(a)
        arrays[f"in_{name}_dram"] = a
        args.append(nc.dram_tensor(f"in_{name}_dram", a.shape, _mybir.dt.from_np(a.dtype), kind="ExternalInput").ap())
    args.append(nc.dram_tensor("out_0_dram", inputs['x'].shape, _mybir.dt.float32, kind="ExternalOutput").ap())
    decoder_kernel(nc, widths, *args)
    r = _run(nc, [arrays], core_ids=[0])
    return r.results[0]["out_0_dram"]
```
